# Optimizing a Trainium2 kernel written in Bass

```python
import jax, jax.numpy as jnp
from jax import lax
import numpy as np

D_MODEL = 1024
BATCH = 1
SEQ = 256
DEPTH = 2

CTX_LEN = 256
GRID_W = 64
N_MOD = 9
D_FF = 2816
FFN_RES = 0.5

POOL_WIDTH = 256
POOL_WINDOWS = (2, 4, 8, 16)
POOL_GROUP = POOL_WIDTH // 4

DN_HEADS = 4
DN_DK = 64
DN_DV = 64
DN_CONV = 5
DN_CHUNK = 64
DN_QK = DN_HEADS * DN_DK
DN_VW = DN_HEADS * DN_DV
DN_CONV_CH = 2 * DN_QK + DN_VW

ATT_HEADS = 8
ATT_KV = 2
ATT_GROUP = ATT_HEADS // ATT_KV
ATT_HD = 64
ATT_BLOCK = 128
ROPE_BASE = 10000.0

N_BRANCH = 3
MIX_WIDTH = POOL_WIDTH + DN_VW + ATT_HEADS * ATT_HD
IN_SPLITS = (POOL_WIDTH, DN_CONV_CH, DN_VW, 4 * DN_HEADS,
             ATT_HEADS * ATT_HD, ATT_KV * ATT_HD, ATT_KV * ATT_HD, N_BRANCH * D_MODEL)
IN_COLS = POOL_WIDTH + DN_CONV_CH + DN_VW + 4 * DN_HEADS + ATT_HEADS * ATT_HD + 2 * ATT_KV * ATT_HD + N_BRANCH * D_MODEL

kernel_name = "hybrid_pool_deltanet_gqa_prefix_dit"

F32 = jnp.float32

def rmsnorm(x, g, eps=1e-6):
    xf = x.astype(F32)
    y = xf * lax.rsqrt(jnp.mean(xf * xf, axis=-1, keepdims=True) + eps)
    return (y * g.astype(F32)).astype(x.dtype)

def l2norm(x, eps=1e-6):
    xf = x.astype(F32)
    return xf * lax.rsqrt(jnp.sum(xf * xf, axis=-1, keepdims=True) + eps)

def modulate(h, shift, scale):
    return h * (1.0 + scale) + shift

def swiglu(h, w_in, w_out):
    gu = h @ w_in
    g, u = jnp.split(gu, 2, axis=-1)
    return (jax.nn.silu(g) * u) @ w_out

def ffn_sublayer(s, m, g_norm, w_in, w_out):
    h = modulate(rmsnorm(s, g_norm), m[0], m[1])
    return s + FFN_RES * m[2] * swiglu(h, w_in, w_out)

def split_cols(h):
    out, o = [], 0
    for w in IN_SPLITS:
        out.append(h[..., o:o + w])
        o += w
    return out

def multiscale_pool(p, w_grp, scale):
    B, L, _ = p.shape
    pf = p.astype(F32)
    cs = jnp.concatenate([jnp.zeros((B, 1, POOL_WIDTH), F32), jnp.cumsum(pf, axis=1)], axis=1)
    t = jnp.arange(L)
    groups = []
    for gi, w in enumerate(POOL_WINDOWS):
        lo = jnp.clip(t - w // 2, 0, L)
        hi = jnp.clip(t + w - w // 2, 0, L)
        sl = slice(gi * POOL_GROUP, (gi + 1) * POOL_GROUP)
        csg = cs[:, :, sl]
        win_sum = csg[:, hi] - csg[:, lo]
        cnt = (hi - lo).astype(F32)[None, :, None]
        groups.append(win_sum / cnt - pf[:, :, sl])
    y = jnp.stack(groups, axis=2).astype(p.dtype)
    y = jnp.einsum('blgi,gio->blgo', y, w_grp).reshape(B, L, POOL_WIDTH)
    return y * scale

def short_conv(x, w):
    C = x.shape[-1]
    y = lax.conv_general_dilated(x, w[:, None, :].astype(x.dtype), window_strides=(1,), padding='SAME',
                                 dimension_numbers=('NWC', 'WIO', 'NWC'), feature_group_count=C)
    return jax.nn.silu(y)

def dn_prepare(qkv, ba, conv_w, a_log, dt_bias):
    B, L, _ = qkv.shape
    qkv = short_conv(qkv, conv_w).astype(F32)
    q = qkv[..., :DN_QK].reshape(B, L, DN_HEADS, DN_DK)
    k = qkv[..., DN_QK:2 * DN_QK].reshape(B, L, DN_HEADS, DN_DK)
    v = qkv[..., 2 * DN_QK:].reshape(B, L, DN_HEADS, DN_DV)
    q = l2norm(q) * (DN_DK ** -0.5)
    k = l2norm(k)
    ba = ba.astype(F32).reshape(B, L, 2, 2, DN_HEADS)
    beta = jax.nn.sigmoid(ba[:, :, 0])
    g = -jnp.exp(a_log.astype(F32)) * jax.nn.softplus(ba[:, :, 1] + dt_bias.astype(F32))
    to_bhl = lambda t: jnp.transpose(t, (0, 2, 1, 3))
    beta = jnp.transpose(beta, (2, 0, 3, 1))
    g = jnp.transpose(g, (2, 0, 3, 1))
    return to_bhl(q), to_bhl(k), to_bhl(v), beta, g

def gated_delta_chunked(q, k, v, beta, g, S0):
    B, H, L, DK = q.shape
    DV = v.shape[-1]
    C = DN_CHUNK
    N = L // C
    q = q.reshape(B, H, N, C, DK)
    k = k.reshape(B, H, N, C, DK)
    v = v.reshape(B, H, N, C, DV)
    beta = beta.reshape(B, H, N, C)
    G = jnp.cumsum(g.reshape(B, H, N, C), axis=-1)
    tril_incl = jnp.tril(jnp.ones((C, C), dtype=bool))
    tril_strict = jnp.tril(jnp.ones((C, C), dtype=bool), -1)
    decay_mat = jnp.exp(jnp.where(tril_incl, G[..., :, None] - G[..., None, :], -jnp.inf))
    kk = jnp.einsum('bhncd,bhnsd->bhncs', k, k)
    A = jnp.where(tril_strict, beta[..., :, None] * kk * decay_mat, 0.0)
    lhs = A + jnp.eye(C, dtype=F32)
    rhs = jnp.concatenate([v * beta[..., None], k * (beta * jnp.exp(G))[..., None]], axis=-1)
    sol = lax.linalg.triangular_solve(lhs, rhs, left_side=True, lower=True, unit_diagonal=True)
    u, w = sol[..., :DV], sol[..., DV:]
    qk = jnp.einsum('bhncd,bhnsd->bhncs', q, k) * decay_mat
    q_dec = q * jnp.exp(G)[..., None]
    k_dec = k * jnp.exp(G[..., -1:] - G)[..., None]
    g_last = jnp.exp(G[..., -1])

    def step(S, xs):
        u_n, w_n, qk_n, qd_n, kd_n, gl_n = xs
        v_new = u_n - jnp.einsum('bhcd,bhde->bhce', w_n, S)
        o_n = jnp.einsum('bhcd,bhde->bhce', qd_n, S) + jnp.einsum('bhcs,bhse->bhce', qk_n, v_new)
        S = S * gl_n[..., None, None] + jnp.einsum('bhcd,bhce->bhde', kd_n, v_new)
        return S, o_n

    xs = tuple(jnp.moveaxis(t, 2, 0) for t in (u, w, qk, q_dec, k_dec, g_last))
    S_final, o = lax.scan(step, S0, xs)
    o = jnp.moveaxis(o, 0, 2).reshape(B, H, L, DV)
    return o, S_final

def bidir_delta(q, k, v, beta, g, S0_f, S0_b):
    flip = lambda t: jnp.flip(t, axis=2)
    o_f, S_f = gated_delta_chunked(q, k, v, beta[0], g[0], S0_f)
    o_b, S_b = gated_delta_chunked(flip(q), flip(k), flip(v), flip(beta[1]), flip(g[1]), S0_b)
    return o_f + flip(o_b), S_f, S_b

def dn_output(o, z, g_norm):
    B, H, L, DV = o.shape
    o = jnp.transpose(o, (0, 2, 1, 3))
    y = rmsnorm(o, g_norm) * jax.nn.silu(z.reshape(B, L, H, DV).astype(F32))
    return y.reshape(B, L, H * DV).astype(z.dtype)

def axial_rope_tables(n_tokens):
    rows = n_tokens // GRID_W
    row = jnp.broadcast_to(jnp.arange(rows)[:, None], (rows, GRID_W)).reshape(-1)
    col = jnp.broadcast_to(jnp.arange(GRID_W)[None, :], (rows, GRID_W)).reshape(-1)
    n_freq = ATT_HD // 4
    inv = ROPE_BASE ** (-jnp.arange(n_freq, dtype=F32) / n_freq)
    ang = jnp.concatenate([row[:, None].astype(F32) * inv, col[:, None].astype(F32) * inv], axis=-1)
    return jnp.cos(ang), jnp.sin(ang)

def apply_rope(x, cos, sin):
    xf = x.astype(F32)
    x1, x2 = xf[..., 0::2], xf[..., 1::2]
    c = cos[None, :, None, :]
    s = sin[None, :, None, :]
    y = jnp.stack([x1 * c - x2 * s, x1 * s + x2 * c], axis=-1).reshape(x.shape)
    return y.astype(x.dtype)

def gqa_softmax(q, k, v):
    s = jnp.einsum('bqkgd,bskd->bkgqs', q, k).astype(F32) * (ATT_HD ** -0.5)
    p = jax.nn.softmax(s, axis=-1).astype(v.dtype)
    return jnp.einsum('bkgqs,bskd->bqkgd', p, v)

def latent_attention(q, k_lat, v_lat, k_ctx, v_ctx):
    B, L = q.shape[:2]
    k_all = jnp.concatenate([k_ctx, k_lat], axis=1)
    v_all = jnp.concatenate([v_ctx, v_lat], axis=1)
    n_blk = L // ATT_BLOCK
    qb = q.reshape(B, n_blk, ATT_BLOCK, ATT_KV, ATT_GROUP, ATT_HD).transpose(1, 0, 2, 3, 4, 5)
    o = lax.map(lambda qblk: gqa_softmax(qblk, k_all, v_all), qb)
    return o.transpose(1, 0, 2, 3, 4, 5).reshape(B, L, ATT_HEADS * ATT_HD)

def context_attention(q, k, v):
    B, Lc = q.shape[:2]
    o = gqa_softmax(q.reshape(B, Lc, ATT_KV, ATT_GROUP, ATT_HD), k, v)
    return o.reshape(B, Lc, ATT_HEADS * ATT_HD)

def split_heads(t, n):
    return t.reshape(t.shape[0], t.shape[1], n, ATT_HD)

def merge_branches(y_pool, y_dn, y_att, gates, w_branch, w_out):
    ga, gb, gc = jnp.split(jax.nn.sigmoid(gates), N_BRANCH, axis=-1)
    wa = w_branch[:POOL_WIDTH]
    wb = w_branch[POOL_WIDTH:POOL_WIDTH + DN_VW]
    wc = w_branch[POOL_WIDTH + DN_VW:]
    m = ga * (y_pool @ wa) + gb * (y_dn @ wb) + gc * (y_att @ wc)
    return m @ w_out

def mixer_sublayer(x, xc, mx, mc, p, ctx_out):
    def project(s, m):
        h = modulate(rmsnorm(s, p["norm_mix"]), m[0], m[1])
        return split_cols(h @ p["w_in"])

    pool_x, qkv_x, z_x, ba_x, aq_x, ak_x, av_x, gate_x = project(x, mx)
    pool_c, qkv_c, z_c, ba_c, aq_c, ak_c, av_c, gate_c = project(xc, mc)

    B = x.shape[0]
    S0 = jnp.zeros((B, DN_HEADS, DN_DK, DN_DV), F32)
    qd_c, kd_c, vd_c, beta_c, g_c = dn_prepare(qkv_c, ba_c, p["dn_conv"], p["dn_a_log"], p["dn_dt_bias"])
    od_c, S_f, S_b = bidir_delta(qd_c, kd_c, vd_c, beta_c, g_c, S0, S0)
    qd_x, kd_x, vd_x, beta_x, g_x = dn_prepare(qkv_x, ba_x, p["dn_conv"], p["dn_a_log"], p["dn_dt_bias"])
    od_x, _, _ = bidir_delta(qd_x, kd_x, vd_x, beta_x, g_x, S_f, S_b)

    cos, sin = axial_rope_tables(x.shape[1])
    q_x = apply_rope(rmsnorm(split_heads(aq_x, ATT_HEADS), p["q_norm"]), cos, sin)
    k_x = apply_rope(rmsnorm(split_heads(ak_x, ATT_KV), p["k_norm"]), cos, sin)
    v_x = split_heads(av_x, ATT_KV)
    k_c = rmsnorm(split_heads(ak_c, ATT_KV), p["k_norm"])
    v_c = split_heads(av_c, ATT_KV)
    att_x = latent_attention(q_x, k_x, v_x, k_c, v_c)

    y_x = merge_branches(multiscale_pool(pool_x, p["pool_w"], p["pool_scale"]),
                         dn_output(od_x, z_x, p["dn_norm"]), att_x, gate_x, p["w_branch"], p["w_out"])
    x = x + mx[2] * y_x
    if ctx_out:
        q_c = rmsnorm(split_heads(aq_c, ATT_HEADS), p["q_norm"])
        att_c = context_attention(q_c, k_c, v_c)
        y_c = merge_branches(multiscale_pool(pool_c, p["pool_w"], p["pool_scale"]),
                             dn_output(od_c, z_c, p["dn_norm"]), att_c, gate_c, p["w_branch"], p["w_out"])
        xc = xc + mc[2] * y_c
    return x, xc

def trunk_layer(x, xc, mod, mod_c, p, ctx_out):
    mx = jnp.split(mod[:, None, :], N_MOD, axis=-1)
    mc = jnp.split(mod_c[:, None, :], N_MOD, axis=-1)
    x = ffn_sublayer(x, mx[0:3], p["norm_ffn1"], p["w_ffn1_in"], p["w_ffn1_out"])
    xc = ffn_sublayer(xc, mc[0:3], p["norm_ffn1"], p["w_ffn1_in"], p["w_ffn1_out"])
    x, xc = mixer_sublayer(x, xc, mx[3:6], mc[3:6], p, ctx_out)
    x = ffn_sublayer(x, mx[6:9], p["norm_ffn2"], p["w_ffn2_in"], p["w_ffn2_out"])
    if ctx_out:
        xc = ffn_sublayer(xc, mc[6:9], p["norm_ffn2"], p["w_ffn2_in"], p["w_ffn2_out"])
    return x, xc

def setup_inputs(seed: int = 0) -> dict:
    key = jax.random.key(seed)
    ks = iter(jax.random.split(key, 40))
    D = D_MODEL
    nrm = lambda shape, scale: jax.random.normal(next(ks), shape, F32) * scale
    gain = lambda shape: 1.0 + nrm(shape, 0.02)
    a_log = jnp.log(jax.random.uniform(next(ks), (DEPTH, 2, DN_HEADS), F32, 1.0, 16.0))
    dt = jnp.exp(jax.random.uniform(next(ks), (DEPTH, 2, DN_HEADS), F32, np.log(1e-3), np.log(1e-1)))
    dt_bias = dt + jnp.log(-jnp.expm1(-dt))
    w_branch = jnp.concatenate([nrm((DEPTH, POOL_WIDTH, D), POOL_WIDTH ** -0.5),
                                nrm((DEPTH, DN_VW, D), DN_VW ** -0.5),
                                nrm((DEPTH, ATT_HEADS * ATT_HD, D), (ATT_HEADS * ATT_HD) ** -0.5)], axis=1)
    return {
        "x": nrm((BATCH, SEQ, D), 1.0),
        "c": nrm((BATCH, D), 1.0),
        "ctx": nrm((BATCH, CTX_LEN, D), 1.0),
        "c_ctx": nrm((D,), 1.0),
        "w_ada": nrm((DEPTH, D, N_MOD * D), 0.5 * D ** -0.5),
        "b_ada": nrm((DEPTH, N_MOD * D), 0.02),
        "norm_ffn1": gain((DEPTH, D)),
        "w_ffn1_in": nrm((DEPTH, D, 2 * D_FF), D ** -0.5),
        "w_ffn1_out": nrm((DEPTH, D_FF, D), D_FF ** -0.5),
        "norm_mix": gain((DEPTH, D)),
        "w_in": nrm((DEPTH, D, IN_COLS), D ** -0.5),
        "pool_w": nrm((DEPTH, 4, POOL_GROUP, POOL_GROUP), POOL_GROUP ** -0.5),
        "pool_scale": gain((DEPTH, POOL_WIDTH)),
        "dn_conv": nrm((DEPTH, DN_CONV, DN_CONV_CH), DN_CONV ** -0.5),
        "dn_a_log": a_log,
        "dn_dt_bias": dt_bias,
        "dn_norm": gain((DEPTH, DN_DV)),
        "q_norm": gain((DEPTH, ATT_HD)),
        "k_norm": gain((DEPTH, ATT_HD)),
        "w_branch": w_branch,
        "w_out": nrm((DEPTH, D, D), D ** -0.5),
        "norm_ffn2": gain((DEPTH, D)),
        "w_ffn2_in": nrm((DEPTH, D, 2 * D_FF), D ** -0.5),
        "w_ffn2_out": nrm((DEPTH, D_FF, D), D_FF ** -0.5),
        "norm_final": gain((D,)),
    }

def reference(x, c, ctx, c_ctx, w_ada, b_ada, norm_ffn1, w_ffn1_in, w_ffn1_out, norm_mix, w_in,
              pool_w, pool_scale, dn_conv, dn_a_log, dn_dt_bias, dn_norm, q_norm, k_norm,
              w_branch, w_out, norm_ffn2, w_ffn2_in, w_ffn2_out, norm_final):
    s_lat = jax.nn.silu(c)
    s_ctx = jax.nn.silu(c_ctx)[None]
    xc = ctx
    for l in range(DEPTH):
        mod = s_lat @ w_ada[l] + b_ada[l]
        mod_c = s_ctx @ w_ada[l] + b_ada[l]
        p = {
            "norm_ffn1": norm_ffn1[l], "w_ffn1_in": w_ffn1_in[l], "w_ffn1_out": w_ffn1_out[l],
            "norm_mix": norm_mix[l], "w_in": w_in[l],
            "pool_w": pool_w[l], "pool_scale": pool_scale[l],
            "dn_conv": dn_conv[l], "dn_a_log": dn_a_log[l], "dn_dt_bias": dn_dt_bias[l], "dn_norm": dn_norm[l],
            "q_norm": q_norm[l], "k_norm": k_norm[l],
            "w_branch": w_branch[l], "w_out": w_out[l],
            "norm_ffn2": norm_ffn2[l], "w_ffn2_in": w_ffn2_in[l], "w_ffn2_out": w_ffn2_out[l],
        }
        x, xc = trunk_layer(x, xc, mod, mod_c, p, ctx_out=(l < DEPTH - 1))
    return rmsnorm(x, norm_final)


_drawn_inputs = setup_inputs


def setup_inputs(seed=0):
    import zlib

    import numpy as np

    out = dict(_drawn_inputs(seed))
    spreads = {}
    factors = {'norm_ffn1': 8.0,
     'norm_mix': 8.0,
     'pool_scale': 8.0,
     'dn_norm': 8.0,
     'q_norm': 8.0,
     'k_norm': 8.0,
     'norm_ffn2': 8.0,
     'norm_final': 2.794}
    for name, (base, spread) in spreads.items():
        noise = np.random.default_rng([zlib.crc32(name.encode()), seed]).standard_normal(out[name].shape)
        drawn = base * np.exp(spread * noise) if base else spread * noise
        out[name] = __import__('jax').numpy.asarray(drawn.astype(out[name].dtype))
    for name, factor in factors.items():
        out[name] = (out[name] * factor).astype(out[name].dtype)
    return out
```

```python
from contextlib import ExitStack

import numpy as np

import concourse.bass as bass
from concourse import mybir

F32 = mybir.dt.float32
F32R = mybir.dt.float32r
ACT = mybir.ActivationFunctionType
ALU = mybir.AluOpType
AXX = mybir.AxisListType.X

P = 128
D = 1024
KD = D // P
LAT, CTX = 256, 256
TOK = LAT + CTX
TT = TOK // P
DEPTH = 2
FF = 2816
KF = FF // P
GRID_W = 64
WINDOWS = (2, 4, 8, 16)
HEADS = 4
HD = 64
QH = 8
TAPS = 5
EPS = 1e-6
N_MOD = 9
ADA = N_MOD * KD
OFF_POOL, OFF_QKV, OFF_Z, OFF_BA, OFF_AQ, OFF_AK, OFF_AV, OFF_GATE = 0, 256, 1024, 1280, 1296, 1808, 1936, 2064

CHUNKS = ((0, 6), (6, 12), (12, 17), (17, 22))
N_FFN = 2 * KF + 4 * KD
N_PROJ = 16
N_MIX = N_PROJ + 4 * KD + KD
FFN_BASE = (0, N_FFN + N_MIX, 2 * N_FFN + N_MIX, 3 * N_FFN + 2 * N_MIX)
MIX_BASE = (N_FFN, 3 * N_FFN + N_MIX)
FFN_STAGE = (0, 2, 3, 5)
MIX_STAGE = (1, 4)
RAW, SPLIT = 4, 2
ADA_FIRST = 3 * KD
ADA_BIG = ADA_FIRST - 2
V_ADA, V_N1, V_NM, V_N2, V_PS, V_CONV, V_DN, V_QN, V_KN = 0, 72, 80, 88, 96, 98, 128, 129, 130
N_VEC = 131
LEVELS = (2, 4, 8, 16, 32, 64)


def names():
    return ["xT", "cT", "w_ada", "w_up", "w_down", "w_proj", "w_ba", "w_merge", "w_out",
            "vecs", "norm_final", "w_pool", "ba_rows", "consts", "pool_mats"]


C_ID, C_SWAP, C_HEADS, C_TRI, C_M1 = 0, 128, 256, 384, 640
C_LV = 896
C_COS = C_LV + len(LEVELS) * 2 * 64
C_SIN = C_COS + LAT
N_CONST = C_SIN + LAT


def build_program(nc, a):
    with ExitStack() as ctx:
        def sb(name, shape, dt=F32, at=ctx):
            return at.enter_context(nc.sbuf_tensor(name, shape, dt))

        def sem(name):
            return ctx.enter_context(nc.semaphore(name))

        class Signal:

            def __init__(self, name, *per_layer):
                self.sem = sem(name)
                self.before = [sum(per_layer[:i]) for i in range(len(per_layer))]

            def at(self, layer, n):
                return self.before[layer] + n

        x = sb("x", [P, KD, TOK])
        h_hi = sb("h_hi", [P, KD, TOK], F32R)
        h_lo = sb("h_lo", [P, KD, TOK], F32R)
        raw = sb("raw", [P, RAW, KD * P])
        w_hi = sb("w_hi", [P, SPLIT, KD * P], F32R)
        w_lo = sb("w_lo", [P, SPLIT, KD * P], F32R)
        ada = sb("ada", [P, 2, KD * P])
        buf_a = sb("buf_a", [P, 2, TOK])
        buf_b = sb("buf_b", [P, 2, TOK])
        rms = sb("rms", [P, TOK])
        inv = sb("inv", [P, TOK])
        consts = sb("consts", [P, N_CONST])
        ones = sb("ones", [P, P])
        eps_col = sb("eps_col", [P, 1])
        one_col = sb("one_col", [P, 1])
        vecs = sb("vecs", [P, DEPTH, N_VEC])
        nfin = sb("nfin", [P, KD])
        c_in = sb("c_in", [P, KD, 2])
        c_act = sb("c_act", [P, KD, 2])
        mod = sb("mod", [P, DEPTH, ADA, 2])
        gain = sb("gain", [P, DEPTH, 3, KD, 2])
        ident = consts[:, C_ID:C_ID + P]
        swap = consts[:, C_SWAP:C_SWAP + P]
        head_ones = consts[:, C_HEADS:C_HEADS + P]
        cos = consts[:, C_COS:C_COS + LAT]
        sin = consts[:, C_SIN:C_SIN + LAT]

        def tri(d):
            return consts[:, C_TRI + d * P:C_TRI + (d + 1) * P]

        def mask_one(d):
            return consts[:, C_M1 + d * P:C_M1 + (d + 1) * P]

        def mask_level(i, d):
            return consts[:, C_LV + (2 * i + d) * 64:C_LV + (2 * i + d + 1) * 64]

        with ExitStack() as s:
            ada_first = sb("ada_first", [P, ADA_BIG, KD * P], at=s)
        with ExitStack() as s:
            a_hi = sb("a_hi", [P, KF, TOK], F32R, at=s)
            a_lo = sb("a_lo", [P, KF, TOK], F32R, at=s)
        with ExitStack() as s:
            out_t = sb("out_t", [P, KD, LAT], at=s)
        mixer = ctx.enter_context(ExitStack())
        qkvT = sb("qkvT", [P, 6, TOK], at=mixer)
        s = ExitStack()
        pre = sb("pre", [P, 2, 2, LAT + 4], at=s)
        conv = sb("conv", [P, 2, TOK], at=s)
        kT = sb("kT", [P, TOK], at=s)
        v_nat = sb("v_nat", [P, TT, P], at=s)
        pool_nat = sb("pool_nat", [P, TT, 2 * P], at=s)
        pool_mats = sb("pool_mats", [P, 2, 4, LAT], at=s)
        pooled = sb("pooled", [P, 2, 2, LAT], at=s)
        prob = sb("prob", [P, 2, TOK], at=s)
        probT = sb("probT", [P, 2, TOK], at=s)
        ba_raw = sb("ba_raw", [P, KD * 16], at=s)
        ba_hi = sb("ba_hi", [P, KD * 16], F32R, at=s)
        ba_lo = sb("ba_lo", [P, KD * 16], F32R, at=s)
        s.close()
        s = ExitStack()
        k_nat = sb("k_nat", [P, TT, 2 * P], at=s)
        vd_nat = sb("vd_nat", [P, TT, 2 * P], at=s)
        amT = sb("amT", [P, 16, P], at=s)
        tm = sb("tm", [P, 16, P], at=s)
        um = sb("um", [P, 16, P], at=s)
        xm = sb("xm", [P, 16, HD], at=s)
        em = sb("em", [P, 2, 4, P], at=s)
        eg = sb("eg", [P, 2, 4, P], at=s)
        qkm = sb("qkm", [P, 16, P], at=s)
        q_dec = sb("q_dec", [P, 2, TOK], at=s)
        wT = sb("wT", [P, 2, TT, P], at=s)
        state = sb("state", [P, 2, HD], at=s)
        vnew = sb("vnew", [P, 2, 2, HD], at=s)
        vtmp = sb("vtmp", [P, 2, 2, HD], at=s)
        s.close()
        s = ExitStack()
        above = sb("above", [P, 15976], at=s)
        ba = sb("ba", [P, TT, 16], at=s)
        ba_rows = sb("ba_rows", [P, 16], at=s)
        beta = sb("beta", [P, TT, 8], at=s)
        gdt = sb("gdt", [P, TT, 8], at=s)
        g_abs = sb("g_abs", [P, TT, 8], at=s)
        g_log = sb("g_log", [P, TT, 8], at=s)
        neg_a = sb("neg_a", [P, 8], at=s)
        g_cum = sb("g_cum", [P, 2, TT, 4], at=s)
        g_exp = sb("g_exp", [P, 2, TT, 4], at=s)
        g_end = sb("g_end", [P, 2, TT, 4], at=s)
        g_state = sb("g_state", [P, 2, TT], at=s)
        w_pool = sb("w_pool", [P, 2, HD], at=s)
        stat = sb("stat", [P, 2, 4], at=s)
        y = sb("y", [P, KD, TOK], at=s)
        s.close()
        oT = qkvT[:, 4:6, :]
        ke = xm
        ub = em[:, :, :, :].rearrange("p a q (b n) -> p (a q b) n", b=2)
        kd = eg[:, :, :, :].rearrange("p a q n -> p a (q n)")[:, :, 0:4 * HD].rearrange("p a (q n) -> p a q n", q=4)
        ps = ctx.enter_context(nc.psum_tensor("ps", [P, 8, 512], F32))
        mod_ps = ps[:, 7, 0:2 * DEPTH * ADA].rearrange("p (t s) -> p t s", s=2)

        s_const = sem("const_loaded")
        s_x = sem("x_loaded")
        s_first = [sem(f"ada_first_loaded{i}") for i in range(3)]
        s_raw = [sem(f"raw_loaded{i}") for i in range(RAW)]
        s_ada = [sem(f"ada_loaded{i}") for i in range(2)]
        s_mixw = sem("mixer_small_loaded")
        s_bar = sem("ba_rows_loaded")
        s_pm = sem("pool_mats_loaded")
        s_out = sem("out_stored")
        s_set = sem("set_up")
        s_cact = sem("c_act_ready")
        s_adad = sem("ada_tiles_done")
        s_mods = sem("mods_ready")
        s_hi = sem("w_hi_ready")
        s_lo = sem("w_lo_ready")
        s_pe = sem("blocks_done")
        s_sq = sem("squares_ready")
        s_squ = sem("squares_used")
        s_sum = sem("sum_ready")
        s_rt = sem("root_ready")
        s_t = sem("scaled_ready")
        s_hhi = sem("h_hi_ready")
        s_h = sem("h_ready")
        s_fin = sem("final_ready")
        s_xr = sem("x_ready")
        s_silu = sem("silu_ready")
        s_mul = sem("hidden_ready")
        s_ahi = sem("a_hi_ready")
        s_alo = sem("a_lo_ready")
        s_down = sem("down_added")
        s_act = sem("act_chain")
        s_vec = sem("vec_chain")
        s_pool = sem("pool_chain")
        bah = Signal("ba_hi_ready", 1, 1)
        bal = Signal("ba_lo_ready", 1, 1)
        bap = Signal("ba_projected", 1, 1)
        bae = Signal("ba_taken", 1, 1)
        pads = Signal("pads_zero", 1, 1)
        evac = Signal("projection_taken", N_PROJ, N_PROJ)
        cnv = Signal("conv_ready", 6, 6)
        qkv = Signal("qkv_ready", 6, 6)
        hsq = Signal("head_squares_ready", 9 + 2, 9 + 2)
        hsum = Signal("head_sums_ready", 9 + 2, 9 + 2)
        hrt = Signal("head_roots_ready", 9 + 2, 9 + 2)
        hn = Signal("head_normed", 9 + 2, 9 + 2)
        swp = Signal("swapped", 5, 5)
        rop = Signal("roped", 5, 5)
        pl1 = Signal("pooled_sum", 2, 1)
        pl2 = Signal("pooled_taken", 2, 1)
        pl3 = Signal("pool_mixed", 2, 1)
        pl4 = Signal("pool_out", 2, 1)
        NAT = (32, 16)
        sco = Signal("scores_ready", *NAT)
        nmx = Signal("max_ready", *NAT)
        exq = Signal("exp_ready", *NAT)
        prb = Signal("prob_ready", *NAT)
        ptr = Signal("prob_transposed", *NAT)
        pte = Signal("probT_ready", *NAT)
        att = Signal("attention_done", *NAT)
        ate = Signal("attention_taken", *NAT)
        bact = Signal("beta_ready", 1, 1)
        gact = Signal("log_ready", 1, 1)
        gab = Signal("dt_ready", 1, 1)
        naa = Signal("neg_a_ready", 1, 1)
        gdy = Signal("g_ready", 1, 1)
        gcp = Signal("g_summed", 1, 1)
        gct = Signal("g_cum_ready", 1, 1)
        gex = Signal("g_exp_ready", 1, 1)
        ntp = Signal("nat_transposed", 4, 4)
        nte = Signal("nat_ready", 4, 4)
        row = Signal("g_rows_ready", 8, 8)
        rowd = Signal("g_rows_read", 8, 8)
        ega = Signal("eg_ready", 8, 8)
        eax = Signal("e_ready", 8, 8)
        edn = Signal("e_used", 8, 8)
        gram = Signal("grams_ready", 4, 4)
        gend = Signal("g_end_ready", 2, 2)
        gendx = Signal("g_end_exp", 2, 2)
        u1 = Signal("u_first_ready", 8, 8)
        NL = len(LEVELS)
        tr0 = Signal("t_first_ready", 4, 4)
        tr0e = Signal("t_first_taken", 4, 4)
        xps = Signal("x_made", 4 * NL, 4 * NL)
        xmk = Signal("x_masked", 4 * NL, 4 * NL)
        yps = Signal("y_made", 4 * NL, 4 * NL)
        tup = Signal("t_updated", 4 * NL, 4 * NL)
        trp = Signal("t_transposed", 4 * NL, 4 * NL)
        upd = Signal("u_updated", 4 * NL, 4 * NL)
        ups = Signal("u_solved", 4, 4)
        ube = Signal("ub_ready", 4, 4)
        keg = Signal("ke_ready", 2, 2)
        wps = Signal("w_made", 4, 4)
        wte = Signal("wT_ready", 4, 4)
        kds = Signal("kd_ready", 8, 8)
        ws = Signal("ws_made", 8, 8)
        vn = Signal("v_new_ready", 8, 8)
        op = Signal("o_made", 8, 8)
        oe = Signal("o_taken", 8, 8)
        su = Signal("state_made", 8, 8)
        st = Signal("state_ready", 10, 10)
        ydn = Signal("y_dn_ready", 1, 1)
        yhi = Signal("y_hi_ready", KD, KD)
        ylo = Signal("y_lo_ready", KD, KD)
        sgm = Signal("gates_ready", 3 * KD, 3 * KD)
        mg = Signal("merged", KD, KD)
        mhi = Signal("m_hi_ready", KD, KD)
        mlo = Signal("m_lo_ready", KD, KD)
        outd = Signal("out_added", KD, KD)

        block = ctx.enter_context(nc.Block())

        def n_tok(f):
            return TOK if f < 3 else LAT

        def halves(n):
            return [(i, slice(i * LAT, (i + 1) * LAT)) for i in range(n // LAT)]

        def ffn_ada(f, down):
            if f > 1:
                return 0, 0
            t0 = ADA_FIRST + f * 60
            return (t0 + 44, 2) if down else (t0, 4)

        def scan_tile(d, t):
            return ((2, 3, 0, 1), (3, 2, 1, 0))[d][t]

        def mods_at(l, which):
            return ((1, 2, 2), (3, 3, 3))[l][which]

        @block.sync
        def _(sp):
            for i in range(3):
                some = slice(i * KD, min((i + 1) * KD, ADA_BIG))
                sp.dma_start(ada_first[:, some, :], a["w_ada"][some].rearrange("t p n -> p t n")).then_inc(s_first[i], 16)

            def load(j, b, src, cols=KD * P, wait=True):
                if wait:
                    sp.wait_ge(s_lo, b - RAW + 1)
                sp.dma_start(raw[:, j, 0:cols], src).then_inc(s_raw[j], 16)

            def load_ada(j, t, wait=True):
                if wait:
                    sp.wait_ge(s_adad, t - 1)
                sp.dma_start(ada[:, j, :], a["w_ada"][t]).then_inc(s_ada[j], 16)

            for t in range(ADA_BIG, ADA_FIRST):
                load_ada(t % 2, t, wait=False)

            def ffn(f):
                b0 = FFN_BASE[f]

                def up(it, wait=True):
                    t0, per = ffn_ada(f, False)
                    for j in range(4):
                        load(j, b0 + 4 * it + j, a["w_up"][f, 4 * it + j], wait=wait)
                        if per:
                            load_ada(j % 2, t0 + 4 * it + j)
                if f == 0:
                    up(0, wait=False)
                with sp.Fori(1 if f == 0 else 0, KF // 2) as it:
                    up(it)
                with sp.Fori(0, KD) as i:
                    t0, per = ffn_ada(f, True)
                    for j, (k0, k1) in enumerate(CHUNKS):
                        load(j, b0 + 2 * KF + 4 * i + j, a["w_down"][f, i, :, k0 * P:k1 * P], (k1 - k0) * P)
                        if per and j % 2:
                            load_ada(j // 2, t0 + 2 * i + j // 2)

            def mix(l):
                b0 = MIX_BASE[l]
                sp.wait_ge(s_xr, MIX_STAGE[l])
                sp.dma_start(ba_raw[:, :], a["w_ba"][l]).then_inc(s_mixw, 16)
                sp.dma_start(w_pool[:, :, :], a["w_pool"][l]).then_inc(s_pm, 16)
                sp.dma_start(ba_rows[:, :], a["ba_rows"][l]).then_inc(s_bar, 16)
                sp.wait_ge(s_pm, 32 * l + 16)
                sp.dma_start(pool_mats[:, :, :, :], a["pool_mats"]).then_inc(s_pm, 16)
                for n in range(N_PROJ):
                    load(n % RAW, b0 + n, a["w_proj"][l, n])
                with sp.Fori(0, KD) as i:
                    for j in range(4):
                        load(j, b0 + N_PROJ + 4 * i + j, a["w_merge"][l, 4 * i + j])
                with sp.Fori(0, KD // 4) as i:
                    for j in range(4):
                        load(j, b0 + N_PROJ + 4 * KD + 4 * i + j, a["w_out"][l, 4 * i + j])

            ffn(0)
            mix(0)
            ffn(1)
            ffn(2)
            mix(1)
            ffn(3)
            sp.wait_ge(s_fin, KD)
            sp.dma_start(a["out"], out_t[:, :, :]).then_inc(s_out, 16)
            sp.wait_ge(s_out, 16)

        @block.gpsimd
        def _(pool):
            pool.memset(ones[:, :], 1.0).then_inc(s_set, 1)
            pool.memset(eps_col[:, :], EPS).then_inc(s_set, 1)
            pool.memset(one_col[:, :], 1.0).then_inc(s_set, 1)
            for l in range(DEPTH):
                for w in range(2):
                    pool.wait_ge(gex.sem, gex.at(l, 1))
                    pool.wait_ge(nte.sem, nte.at(l, 4))
                    pool.wait_ge(yps.sem, yps.at(l, 2 * NL * (w + 1)))
                    for d in range(2):
                        for e in range(2):
                            h = 2 * w + e
                            last = pool.tensor_tensor(
                                ke[:, 8 * d + e:8 * d + 8:2, :], k_nat[:, :, h * HD:(h + 1) * HD],
                                g_exp[:, d, :, h:h + 1].to_broadcast([P, TT, HD]), ALU.mult)
                    last.then_inc(keg.sem, 1)
                    for t in range(4):
                        n = 4 * w + t
                        if t >= 2:
                            pool.wait_ge(su.sem, su.at(l, n - 1))
                        elif w:
                            pool.wait_ge(su.sem, su.at(l, 3 + t))
                        pool.wait_ge(gendx.sem, gendx.at(l, w + 1))
                        for d in range(2):
                            tt = scan_tile(d, t)
                            last = pool.tensor_tensor(
                                kd[:, t % 2, 2 * d:2 * d + 2, :],
                                k_nat[:, tt, 2 * w * HD:(2 * w + 2) * HD].rearrange("p (e n) -> p e n", e=2),
                                g_end[:, d, tt, 2 * w:2 * w + 2].rearrange("p (e o) -> p e o", o=1)
                                .to_broadcast([P, 2, HD]), ALU.mult)
                        last.then_inc(kds.sem, 1)

        @block.scalar
        def _(act):
            chain = [0]

            def link(ins):
                chain[0] += 1
                ins.then_inc(s_act, 1)
                act.wait_ge(s_act, chain[0])

            act.dma_start(c_in[:, :, :], a["cT"]).then_inc(s_const, 16)
            act.wait_ge(s_const, 16)
            act.dma_start(vecs[:, :, :], a["vecs"]).then_inc(s_const, 16)
            act.dma_start(nfin[:, :], a["norm_final"]).then_inc(s_x, 16)
            act.wait_ge(s_x, 16)
            act.dma_start(x[:, :, :], a["xT"]).then_inc(s_x, 16)
            act.wait_ge(s_const, 32)
            act.dma_start(consts[:, :], a["consts"]).then_inc(s_const, 16)
            act.activation(c_act[:, :, :], c_in[:, :, :], ACT.Silu).then_inc(s_cact, 1)
            act.wait_ge(s_x, 32)
            act.wait_ge(s_set, 3)

            def cast(j, b, cols=KD * P, free=True):
                if free:
                    act.wait_ge(s_pe, b - SPLIT + 1)
                return act.activation(w_hi[:, j % SPLIT, 0:cols], raw[:, j, 0:cols], ACT.Copy)

            def landed(j, base, it=0):
                act.wait_ge(s_raw[j], 16 * (base // RAW + 1) + 16 * it)

            def norm(s, l, which, n):
                if s:
                    act.wait_ge(s_xr, s)
                for k in range(KD):
                    if k >= 2:
                        act.wait_ge(s_squ, (KD - 1) * s + k - 1)
                    act.activation(buf_a[:, k % 2, 0:n], x[:, k, 0:n], ACT.Square).then_inc(s_sq, 1)
                act.wait_ge(s_sum, s + 1)
                act.activation(rms[:, 0:n], ps[:, 6, 0:n], ACT.Sqrt, bias=eps_col[:, 0:1],
                               scale=1.0 / D).then_inc(s_rt, 1)
                if which < 3:
                    act.wait_ge(s_mods, mods_at(l, which))
                for k in range(KD):
                    act.wait_ge(s_t, KD * s + k + 1)
                    if which == 3:
                        act.activation(out_t[:, k, :], buf_a[:, k % 2, 0:n], ACT.Identity,
                                       scale=nfin[:, k:k + 1]).then_inc(s_fin, 1)
                        continue
                    if k >= 2:
                        act.wait_ge(s_h, KD * s + k - 1)
                    for i, cols in halves(n):
                        last = act.activation(buf_b[:, k % 2, cols], buf_a[:, k % 2, cols], ACT.Identity,
                                              bias=mod[:, l, 3 * which * KD + k, i:i + 1],
                                              scale=gain[:, l, which, k, i:i + 1])
                    link(last)
                    act.activation(h_hi[:, k, 0:n], buf_b[:, k % 2, 0:n], ACT.Copy).then_inc(s_hhi, 1)

            def ffn(f):
                n = n_tok(f)
                b0, p0 = FFN_BASE[f], f * KF

                def finish(q, j):
                    def silu():
                        act.wait_ge(s_pe, b0 + 2 * q + 1)
                        act.activation(buf_a[:, j, 0:n], ps[:, 2 * j, 0:n], ACT.Silu).then_inc(s_silu, 1)

                    def upper():
                        act.wait_ge(s_mul, p0 + q + 1)
                        act.activation(a_hi[:, q, 0:n], buf_b[:, j, 0:n], ACT.Copy).then_inc(s_ahi, 1)
                    return silu, upper

                def pair(q, j, it=0, first=False):
                    silu, upper = (None, None) if first else finish(q - 1, 1 - j)
                    for m in range(2):
                        landed(2 * j + m, b0, it)
                        b = b0 + 2 * q + m
                        cast(2 * j + m, b, free=not (isinstance(b, int) and b < SPLIT)).then_inc(s_hi, 1)
                        if not first:
                            (silu, upper)[m]()

                pair(0, 0, first=True)
                with act.Fori(0, KF // 2 - 1) as it:
                    pair(2 * it + 1, 1, it)
                    pair(2 * it + 2, 0, it + 1)
                pair(KF - 1, 1, KF // 2 - 1)
                silu, upper = finish(KF - 1, 1)
                silu()
                upper()
                with act.Fori(0, KD) as i:
                    for j, (k0, k1) in enumerate(CHUNKS):
                        landed(j, b0 + 2 * KF, i)
                        cast(j, b0 + 2 * KF + 4 * i + j, (k1 - k0) * P).then_inc(s_hi, 1)

            def mixer_act(l):
                b0, no = MIX_BASE[l], (TOK, LAT)[l]
                act.wait_ge(s_mixw, 16 * (l + 1))
                act.activation(ba_hi[:, :], ba_raw[:, :], ACT.Copy).then_inc(bah.sem, 1)

                def take(n):
                    act.wait_ge(s_pe, b0 + n + 1)
                    bank = ps[:, n % 2, :]
                    if n < 6:
                        if n >= 2:
                            act.wait_ge(cnv.sem, cnv.at(l, n - 1))
                        else:
                            act.wait_ge(pads.sem, pads.at(l, 1))
                        ins = act.activation(pre[:, n % 2, :, 2:2 + LAT],
                                             bank.rearrange("p (s n) -> p s n", s=2), ACT.Copy)
                    elif n == 6:
                        ins = act.activation(kT[:, :], bank, ACT.Copy)
                    elif n == 7:
                        ins = act.activation(v_nat[:, :, :], bank.rearrange("p (t n) -> p t n", t=TT), ACT.Copy)
                    elif n < 10:
                        ins = act.activation(pool_nat[:, 0:no // P, (n - 8) * P:(n - 7) * P],
                                             bank[:, 0:no].rearrange("p (t n) -> p t n", n=P), ACT.Copy)
                    elif n < 12:
                        ins = act.activation(y[:, 2 + n - 10, 0:no], bank[:, 0:no], ACT.Silu)
                    else:
                        ins = act.activation(y[:, 4 + n - 12, 0:no], bank[:, 0:no], ACT.Copy)
                    ins.then_inc(evac.sem, 1)

                for n in range(N_PROJ):
                    landed(n % RAW, b0 + n - n % RAW)
                    cast(n % RAW, b0 + n).then_inc(s_hi, 1)
                    if n >= 1:
                        take(n - 1)
                    if 0 <= n - 3 < 6:
                        j = n - 3
                        act.wait_ge(cnv.sem, cnv.at(l, j + 1))
                        act.activation(qkvT[:, j, :], conv[:, j % 2, :], ACT.Silu).then_inc(qkv.sem, 1)
                take(N_PROJ - 1)

                act.wait_ge(bae.sem, bae.at(l, 1))
                act.activation(beta[:, :, :], ba[:, :, 0:8], ACT.Sigmoid).then_inc(bact.sem, 1)
                act.wait_ge(s_bar, 16 * (l + 1))
                act.activation(neg_a[:, :], ba_rows[:, 8:16], ACT.Exp).then_inc(naa.sem, 1)
                act.wait_ge(gab.sem, gab.at(l, 1))
                link(act.activation(g_abs[:, :, :], gdt[:, :, :], ACT.Abs))
                link(act.activation(g_log[:, :, :], g_abs[:, :, :], ACT.Exp, scale=-1.0))
                act.activation(g_abs[:, :, :], g_log[:, :, :], ACT.Ln, bias=one_col[:, 0:1]).then_inc(gact.sem, 1)

                def norm_in(l, i):
                    if i < 4:
                        return qkvT[:, i, :], TOK, 1.0
                    if i == 4:
                        return kT[:, :], TOK, 1.0 / HD
                    if i < 9:
                        return y[:, i - 1, 0:no], no, 1.0 / HD
                    return oT[:, i - 9, 0:no], no, 1.0 / HD

                def head_norms(lo, hi):
                    for i in range(lo, hi + 1):
                        if i < hi:
                            src, n, _ = norm_in(l, i)
                            if i - lo >= 2:
                                act.wait_ge(hsum.sem, hsum.at(l, i - 1))
                            act.activation(buf_a[:, i % 2, 0:n], src, ACT.Square).then_inc(hsq.sem, 1)
                        if i > lo:
                            _, n, mean = norm_in(l, i - 1)
                            act.wait_ge(hsum.sem, hsum.at(l, i))
                            if i - 1 - lo >= 2:
                                act.wait_ge(hn.sem, hn.at(l, i - 2))
                            act.activation(buf_b[:, (i - 1) % 2, 0:n], ps[:, (i - 1) % 2, 0:n], ACT.Sqrt,
                                           bias=eps_col[:, 0:1], scale=mean).then_inc(hrt.sem, 1)

                act.wait_ge(qkv.sem, qkv.at(l, 6))
                act.wait_ge(evac.sem, evac.at(l, N_PROJ))
                head_norms(0, 9)

                for s in range(no // LAT):
                    act.wait_ge(pl1.sem, pl1.at(l, s + 1))
                    act.activation(pooled[:, s, :, :], ps[:, 4, :].rearrange("p (t n) -> p t n", t=2),
                                   ACT.Copy).then_inc(pl2.sem, 1)
                    act.wait_ge(pl3.sem, pl3.at(l, s + 1))
                    for t in range(2):
                        last = act.activation(y[:, t, s * LAT:(s + 1) * LAT], ps[:, 5, t * LAT:(t + 1) * LAT],
                                              ACT.Copy, scale=vecs[:, l, V_PS + t:V_PS + t + 1])
                    last.then_inc(pl4.sem, 1)

                N = NAT[l]
                for n in range(N + 1):
                    if n < N:
                        keys = slice(0, TOK) if n < 16 else slice(LAT, TOK)
                        act.wait_ge(nmx.sem, nmx.at(l, n + 1))
                        act.activation(prob[:, n % 2, keys], ps[:, n % 2, keys], ACT.Exp,
                                       bias=stat[:, n % 2, 1:2], scale=HD ** -0.5,
                                       accum_out=stat[:, n % 2, 2:3]).then_inc(exq.sem, 1)
                    if n >= 1:
                        keys = slice(0, TOK) if n - 1 < 16 else slice(LAT, TOK)
                        act.wait_ge(ptr.sem, ptr.at(l, n))
                        if n >= 3:
                            act.wait_ge(att.sem, att.at(l, n - 2))
                        act.activation(probT[:, (n - 1) % 2, keys], ps[:, 2 + (n - 1) % 2, keys],
                                       ACT.Copy).then_inc(pte.sem, 1)

                for j in range(4):
                    act.wait_ge(ntp.sem, ntp.at(l, j + 1))
                    dst = (k_nat, vd_nat)[j // 2]
                    act.activation(dst[:, :, (j % 2) * P:(j % 2 + 1) * P],
                                   ps[:, j % 2, :].rearrange("p (t n) -> p t n", t=TT), ACT.Copy).then_inc(nte.sem, 1)
                act.wait_ge(gct.sem, gct.at(l, 1))
                act.activation(g_exp[:, :, :, :], g_cum[:, :, :, :], ACT.Exp).then_inc(gex.sem, 1)
                for w in range(2):
                    for i in range(4):
                        n = 4 * w + i
                        act.wait_ge(row.sem, row.at(l, n + 1))
                        if i >= 2:
                            act.wait_ge(edn.sem, edn.at(l, n - 1))
                        act.activation(eg[:, i % 2, :, :], ps[:, 2 + i % 2, :].rearrange("p (q n) -> p q n", q=4),
                                       ACT.Exp).then_inc(ega.sem, 1)
                        act.wait_ge(rowd.sem, rowd.at(l, n + 1))
                        act.activation(em[:, i % 2, :, :], em[:, i % 2, :, :], ACT.Exp).then_inc(eax.sem, 1)
                    act.wait_ge(gend.sem, gend.at(l, w + 1))
                    act.activation(g_end[:, :, :, 2 * w:2 * w + 2], g_end[:, :, :, 2 * w:2 * w + 2], ACT.Exp)
                    act.activation(g_state[:, :, :], g_state[:, :, :], ACT.Exp).then_inc(gendx.sem, 1)
                    for d in range(2):
                        act.wait_ge(tr0.sem, tr0.at(l, 2 * w + d + 1))
                        act.activation(tm[:, 8 * d:8 * d + 8, :],
                                       ps[:, 2 + 2 * d:4 + 2 * d, :].rearrange("p b (q n) -> p (b q) n", q=4),
                                       ACT.Copy).then_inc(tr0e.sem, 1)
                    for i, b in enumerate(LEVELS):
                        for d in range(2):
                            n = 2 * NL * w + 2 * i + d
                            act.wait_ge(trp.sem, trp.at(l, n + 1))
                            new = slice(b * (1 - d), b * (2 - d))
                            for m in range(2):
                                q = 8 * d + 4 * m
                                u = um[:, q:q + 4, :].rearrange("p q (i c) -> p q i c", c=2 * b)
                                v = ps[:, 2 + 2 * d + m, :].rearrange("p (q i c) -> p q i c", q=4, c=2 * b)
                                last = act.activation(u[:, :, :, new], v[:, :, :, new], ACT.Copy)
                            last.then_inc(upd.sem, 1)
                    for d in range(2):
                        act.wait_ge(wps.sem, wps.at(l, 2 * w + d + 1))
                        act.activation(wT[:, d, :, :], ps[:, 2 + d, :].rearrange("p (t n) -> p t n", t=TT),
                                       ACT.Copy).then_inc(wte.sem, 1)
                act.wait_ge(oe.sem, oe.at(l, 8))
                head_norms(9, 11)

                act.wait_ge(ydn.sem, ydn.at(l, 1))
                act.wait_ge(ate.sem, ate.at(l, N))
                for k in range(KD):
                    act.activation(a_hi[:, KD + k, 0:no], y[:, k, 0:no], ACT.Copy).then_inc(yhi.sem, 1)

                def turn(i, first=False):
                    for j in range(4):
                        landed(j, b0 + N_PROJ, i)
                        cast(j, b0 + N_PROJ + 4 * i + j).then_inc(s_hi, 1)
                        if j == 2 and not first:
                            act.wait_ge(mg.sem, mg.at(l, i))
                            act.activation(a_hi[:, i - 1, 0:no], buf_b[:, 0, 0:no], ACT.Copy).then_inc(mhi.sem, 1)
                        if j >= 1:
                            if j == 1 and not first:
                                act.wait_ge(mg.sem, mg.at(l, i))
                            act.wait_ge(s_pe, b0 + N_PROJ + 4 * i + j)
                            dst = (buf_a[:, 0, 0:no], buf_a[:, 1, 0:no], buf_b[:, 1, 0:no])[j - 1]
                            act.activation(dst, ps[:, j - 1, 0:no], ACT.Sigmoid).then_inc(sgm.sem, 1)
                turn(0, first=True)
                with act.Fori(1, KD) as i:
                    turn(i)
                act.wait_ge(mg.sem, mg.at(l, KD))
                act.activation(a_hi[:, KD - 1, 0:no], buf_b[:, 0, 0:no], ACT.Copy).then_inc(mhi.sem, 1)
                with act.Fori(0, KD // 4) as i:
                    for j in range(4):
                        landed(j, b0 + N_PROJ + 4 * KD, i)
                        cast(j, b0 + N_PROJ + 4 * KD + 4 * i + j).then_inc(s_hi, 1)

            norm(0, 0, 0, TOK)
            ffn(0)
            norm(1, 0, 1, TOK)
            mixer_act(0)
            norm(2, 0, 2, TOK)
            ffn(1)
            norm(3, 1, 0, TOK)
            ffn(2)
            norm(4, 1, 1, TOK)
            mixer_act(1)
            norm(5, 1, 2, LAT)
            ffn(3)
            norm(6, 0, 3, LAT)

        @block.vector
        def _(vec):
            chain = [0]

            def link(ins):
                chain[0] += 1
                ins.then_inc(s_vec, 1)
                vec.wait_ge(s_vec, chain[0])

            def modulations(l, g0, g1, tiles):
                vec.wait_ge(s_adad, tiles)
                vec.wait_ge(s_const, 48)
                t0, t1 = g0 * KD, g1 * KD
                link(vec.tensor_tensor(
                    mod[:, l, t0:t1, :],
                    mod_ps[:, ADA * l + t0:ADA * l + t1, :],
                    vecs[:, l, t0:t1].rearrange("p (t o) -> p t o", o=1).to_broadcast([P, t1 - t0, 2]), ALU.add))
                for which in range(g0 // 3, g1 // 3):
                    g = V_N1 + which * KD
                    link(vec.scalar_tensor_tensor(
                        gain[:, l, which, :, :], mod[:, l, (3 * which + 1) * KD:(3 * which + 2) * KD, :], 1.0,
                        vecs[:, l, g:g + KD].rearrange("p (t o) -> p t o", o=1).to_broadcast([P, KD, 2]),
                        ALU.add, ALU.mult))
                    if which != 1:
                        gate = mod[:, l, (3 * which + 2) * KD:(3 * which + 3) * KD, :]
                        link(vec.tensor_scalar(gate, gate, 0.5, None, ALU.mult))
                vec.engine_nop().then_inc(s_mods, 1)

            def norm(s, n, final=False):
                vec.wait_ge(s_rt, s + 1)
                link(vec.reciprocal(inv[:, 0:n], rms[:, 0:n]))

                def scaled(k):
                    if k >= 2:
                        vec.wait_ge(s_fin if final else s_hhi, (0 if final else KD * s) + k - 1)
                    vec.tensor_tensor(buf_a[:, k % 2, 0:n], x[:, k, 0:n], inv[:, 0:n], ALU.mult).then_inc(s_t, 1)

                scaled(0)
                for k in range(KD):
                    if k + 1 < KD:
                        scaled(k + 1)
                    if not final:
                        vec.wait_ge(s_hhi, KD * s + k + 1)
                        vec.tensor_tensor(h_lo[:, k, 0:n], buf_b[:, k % 2, 0:n], h_hi[:, k, 0:n].bitcast(F32),
                                          ALU.subtract).then_inc(s_h, 1)

            def lower(j, b, cols=KD * P):
                vec.wait_ge(s_hi, b + 1)
                vec.tensor_tensor(w_lo[:, j % SPLIT, 0:cols], raw[:, j, 0:cols],
                                  w_hi[:, j % SPLIT, 0:cols].bitcast(F32), ALU.subtract).then_inc(s_lo, 1)

            def add_to_x(k, bank, n, l, which):
                for i, cols in halves(n):
                    last = vec.scalar_tensor_tensor(x[:, k, cols], ps[:, bank, cols],
                                                    mod[:, l, (3 * which + 2) * KD + k, i:i + 1], x[:, k, cols],
                                                    ALU.mult, ALU.add)
                return last

            def ffn(f):
                n, l, which = n_tok(f), f // 2, 2 * (f % 2)
                b0, p0 = FFN_BASE[f], f * KF

                def finish(q, j):
                    vec.wait_ge(s_pe, b0 + 2 * q + 2)
                    vec.wait_ge(s_silu, p0 + q + 1)
                    vec.tensor_tensor(buf_b[:, j, 0:n], buf_a[:, j, 0:n], ps[:, 2 * j + 1, 0:n],
                                      ALU.mult).then_inc(s_mul, 1)
                    vec.wait_ge(s_ahi, p0 + q + 1)
                    vec.tensor_tensor(a_lo[:, q, 0:n], buf_b[:, j, 0:n], a_hi[:, q, 0:n].bitcast(F32),
                                      ALU.subtract).then_inc(s_alo, 1)

                def pair(q, j, first=False):
                    for m in range(2):
                        lower(2 * j + m, b0 + 2 * q + m)
                    if not first:
                        finish(q - 1, 1 - j)

                pair(0, 0, True)
                with vec.Fori(0, KF // 2 - 1) as it:
                    pair(2 * it + 1, 1)
                    pair(2 * it + 2, 0)
                pair(KF - 1, 1)
                finish(KF - 1, 1)
                bd = b0 + 2 * KF

                def turn(i, j, first=False):
                    for m, (k0, k1) in enumerate(CHUNKS):
                        lower(m, bd + 4 * i + m, (k1 - k0) * P)
                        if m == 1 and not first:
                            vec.wait_ge(s_pe, bd + 4 * i)
                            add_to_x(i - 1, 4 + j, n, l, which).then_inc(s_down, 1)
                turn(0, 1, True)
                turn(1, 0)
                with vec.Fori(1, KD // 2) as it:
                    turn(2 * it, 1)
                    turn(2 * it + 1, 0)
                vec.wait_ge(s_pe, bd + 4 * KD)
                add_to_x(KD - 1, 5, n, l, which).then_inc(s_down, 1)
                vec.engine_nop().then_inc(s_xr, 1)

            def mixer_vec(l):
                b0, no = MIX_BASE[l], (TOK, LAT)[l]
                vec.memset(pre[:, :, :, 0:2], 0.0)
                vec.memset(pre[:, :, :, 2 + LAT:4 + LAT], 0.0).then_inc(pads.sem, 1)
                vec.wait_ge(bah.sem, bah.at(l, 1))
                vec.tensor_tensor(ba_lo[:, :], ba_raw[:, :], ba_hi[:, :].bitcast(F32),
                                  ALU.subtract).then_inc(bal.sem, 1)

                def convolve(j):
                    vec.wait_ge(evac.sem, evac.at(l, j + 1))
                    if j >= 2:
                        vec.wait_ge(qkv.sem, qkv.at(l, j - 1))
                    dst = conv[:, j % 2, :].rearrange("p (s n) -> p s n", s=2)
                    for i in range(TAPS):
                        w = vecs[:, l, V_CONV + TAPS * j + i:V_CONV + TAPS * j + i + 1]
                        src = pre[:, j % 2, :, i:i + LAT]
                        if i == 0:
                            link(vec.tensor_scalar(dst, src, w, None, ALU.mult))
                        elif i < TAPS - 1:
                            link(vec.scalar_tensor_tensor(dst, src, w, dst, ALU.mult, ALU.add))
                        else:
                            vec.scalar_tensor_tensor(dst, src, w, dst, ALU.mult, ALU.add).then_inc(cnv.sem, 1)

                for n in range(N_PROJ):
                    lower(n % RAW, b0 + n)
                    if n == 0:
                        vec.wait_ge(bap.sem, bap.at(l, 1))
                        vec.tensor_copy(ba[:, :, :], ps[:, 6, 0:TT * 16].rearrange("p (t n) -> p t n", t=TT)
                                        ).then_inc(bae.sem, 1)
                        vec.wait_ge(s_bar, 16 * (l + 1))
                        vec.wait_ge(bae.sem, bae.at(l, 1))
                        vec.tensor_tensor(gdt[:, :, :], ba[:, :, 8:16],
                                          ba_rows[:, 0:8].rearrange("p (o n) -> p o n", o=1)
                                          .to_broadcast([P, TT, 8]), ALU.add).then_inc(gab.sem, 1)
                    if 0 <= n - 2 < 6:
                        convolve(n - 2)

                vec.wait_ge(gab.sem, gab.at(l, 1))
                vec.wait_ge(gact.sem, gact.at(l, 1))
                vec.wait_ge(naa.sem, naa.at(l, 1))
                link(vec.scalar_tensor_tensor(gdt[:, :, :], gdt[:, :, :], 0.0, g_abs[:, :, :], ALU.max, ALU.add))
                vec.scalar_tensor_tensor(gdt[:, :, :], gdt[:, :, :], -1.0,
                                         neg_a[:, :].rearrange("p (o n) -> p o n", o=1).to_broadcast([P, TT, 8]),
                                         ALU.mult, ALU.mult).then_inc(gdy.sem, 1)

                def normed(i):
                    if i < 4:
                        dst, n, f = qkvT[:, i, :], TOK, HD ** -0.5 if i < 2 else 1.0
                    elif i == 4:
                        dst, n, f = kT[:, :], TOK, vecs[:, l, V_KN:V_KN + 1]
                    elif i < 9:
                        dst, n, f = y[:, i - 1, 0:no], no, vecs[:, l, V_QN:V_QN + 1]
                    else:
                        dst, n, f = oT[:, i - 9, 0:no], no, vecs[:, l, V_DN:V_DN + 1]
                    vec.wait_ge(hrt.sem, hrt.at(l, i + 1))
                    if i:
                        vec.wait_ge(hn.sem, hn.at(l, i))
                    link(vec.reciprocal(inv[:, 0:n], buf_b[:, i % 2, 0:n]))
                    vec.scalar_tensor_tensor(dst, dst, f, inv[:, 0:n], ALU.mult, ALU.mult).then_inc(hn.sem, 1)

                def rope(i):
                    dst = kT[:, 0:LAT] if i == 4 else y[:, i - 1, 0:LAT]
                    vec.wait_ge(hn.sem, hn.at(l, i + 1))
                    vec.wait_ge(swp.sem, swp.at(l, i - 3))
                    if i > 4:
                        vec.wait_ge(rop.sem, rop.at(l, i - 4))
                    link(vec.tensor_tensor(rms[:, 0:LAT], ps[:, 2 + i % 2, 0:LAT], sin, ALU.mult))
                    link(vec.tensor_tensor(rms[:, LAT:TOK], dst, cos, ALU.mult))
                    vec.tensor_tensor(dst, rms[:, 0:LAT], rms[:, LAT:TOK], ALU.add).then_inc(rop.sem, 1)

                for i in range(9):
                    normed(i)
                    if i - 1 >= 4:
                        rope(i - 1)
                rope(8)

                N = NAT[l]

                def maximum(n):
                    keys = slice(0, TOK) if n < 16 else slice(LAT, TOK)
                    vec.wait_ge(sco.sem, sco.at(l, n + 1))
                    link(vec.tensor_reduce(stat[:, n % 2, 0:1], ps[:, n % 2, keys], AXX, ALU.max))
                    vec.tensor_scalar(stat[:, n % 2, 1:2], stat[:, n % 2, 0:1], -(HD ** -0.5), None,
                                      ALU.mult).then_inc(nmx.sem, 1)

                def head_of(n):
                    h = n % 8
                    rows = slice((h // 4) * HD, (h // 4 + 1) * HD)
                    return rows, h % 4, slice((n // 8) * P, (n // 8 + 1) * P)

                for n in range(N + 2):
                    if n < N:
                        maximum(n)
                    if 1 <= n <= N:
                        m = n - 1
                        keys = slice(0, TOK) if m < 16 else slice(LAT, TOK)
                        vec.wait_ge(exq.sem, exq.at(l, m + 1))
                        link(vec.reciprocal(stat[:, m % 2, 3:4], stat[:, m % 2, 2:3]))
                        vec.tensor_scalar(prob[:, m % 2, keys], prob[:, m % 2, keys], stat[:, m % 2, 3:4], None,
                                          ALU.mult).then_inc(prb.sem, 1)
                    if n >= 2:
                        m = n - 2
                        rows, t, cols = head_of(m)
                        vec.wait_ge(att.sem, att.at(l, m + 1))
                        vec.tensor_copy(y[rows, 4 + t, cols], ps[rows, 4 + m % 2, 0:P]).then_inc(ate.sem, 1)

                vec.wait_ge(gcp.sem, gcp.at(l, 1))
                vec.tensor_copy(g_cum[:, :, :, :], ps[:, 6, 0:2 * TT * 4].rearrange("p (d t h) -> p d t h", d=2, t=TT)
                                ).then_inc(gct.sem, 1)
                vec.wait_ge(gct.sem, gct.at(l, 1))
                for w in range(2):
                    if w:
                        vec.wait_ge(su.sem, su.at(l, 4))
                    for i in range(4):
                        n, d, t0 = 4 * w + i, i // 2, 2 * (i % 2)
                        rows4 = ps[:, 2 + i % 2, :].rearrange("p (q n) -> p q n", q=4)
                        end = P - 1 if d == 0 else 0
                        vec.wait_ge(row.sem, row.at(l, n + 1))
                        vec.wait_ge(ega.sem, ega.at(l, n + 1))
                        if i >= 2:
                            vec.wait_ge(edn.sem, edn.at(l, n - 1))
                        for q in range(4):
                            g = g_cum[:, d, t0 + q // 2, 2 * w + q % 2:2 * w + q % 2 + 1]
                            vec.tensor_scalar(em[:, i % 2, q, :], rows4[:, q, :], g, 0.0, ALU.subtract, ALU.min)
                        last4 = rows4[:, :, end:end + 1].rearrange("p (t e) o -> p t (e o)", t=2)
                        link(vec.tensor_tensor(g_end[:, d, t0:t0 + 2, 2 * w:2 * w + 2], last4,
                                               g_cum[:, d, t0:t0 + 2, 2 * w:2 * w + 2], ALU.subtract))
                        for e in range(2):
                            r = slice(e * HD, (e + 1) * HD)
                            link(vec.tensor_copy(g_state[r, d, t0:t0 + 2], last4[r, :, e]))
                        vec.engine_nop().then_inc(rowd.sem, 1)
                        cols = slice(t0 * P, (t0 + 2) * P)
                        for e in range(2):
                            r = slice(e * HD, (e + 1) * HD)
                            vec.tensor_tensor(
                                q_dec[r, d, cols].rearrange("p (t n) -> p t n", t=2),
                                qkvT[r, w, cols].rearrange("p (t n) -> p t n", t=2),
                                eg[r, i % 2, e:4:2, :], ALU.mult)
                        vec.wait_ge(eax.sem, eax.at(l, n + 1))
                        vec.wait_ge(gram.sem, gram.at(l, 2 * w + 2))
                        vec.wait_ge(bact.sem, bact.at(l, 1))
                        qk = ps[:, 0:2, cols].rearrange("p e (t n) -> p t e n", t=2)
                        q0 = 8 * d + 4 * (i % 2)
                        for q in range(4):
                            bcol = d * 4 + 2 * w + q % 2
                            last = vec.scalar_tensor_tensor(
                                amT[:, q0 + q, :], ps[:, 4 + q % 2, (t0 + q // 2) * P:(t0 + q // 2 + 1) * P], beta[:, t0 + q // 2, bcol:bcol + 1],
                                em[:, i % 2, q, :], ALU.mult, ALU.mult)
                        link(last)
                        link(vec.tensor_tensor(
                            qkm[:, q0:q0 + 4, :].rearrange("p (t e) n -> p t e n", e=2), qk,
                            em[:, i % 2, :, :].rearrange("p (t e) n -> p t e n", e=2), ALU.mult))
                        link(vec.tensor_tensor(
                            um[:, q0:q0 + 4, :], amT[:, q0:q0 + 4, :],
                            mask_one(d).rearrange("p (o n) -> p o n", o=1).to_broadcast([P, 4, P]), ALU.mult))
                        vec.tensor_tensor(
                            qkm[:, q0:q0 + 4, :], qkm[:, q0:q0 + 4, :],
                            tri(d).rearrange("p (o n) -> p o n", o=1).to_broadcast([P, 4, P]),
                            ALU.mult).then_inc(edn.sem, 1)
                        vec.tensor_tensor(
                            um[:, q0:q0 + 4, :],
                            ident.rearrange("p (o n) -> p o n", o=1).to_broadcast([P, 4, P]),
                            um[:, q0:q0 + 4, :], ALU.subtract).then_inc(u1.sem, 1)
                    vec.engine_nop().then_inc(gend.sem, 1)

                    for i, b in enumerate(LEVELS):
                        for d in range(2):
                            n = 2 * NL * w + 2 * i + d
                            vec.wait_ge(xps.sem, xps.at(l, n + 1))
                            vec.tensor_tensor(
                                xm[:, 8 * d:8 * d + 8, :], ps[:, d, :].rearrange("p (q n) -> p q n", q=8),
                                mask_level(i, d).rearrange("p (o n) -> p o n", o=1).to_broadcast([P, 8, 64]),
                                ALU.mult).then_inc(xmk.sem, 1)
                        for d in range(2):
                            n = 2 * NL * w + 2 * i + d
                            vec.wait_ge(yps.sem, yps.at(l, n + 1))
                            vec.wait_ge(tr0e.sem, tr0e.at(l, 2 * w + d + 1))
                            old = slice(b * d, b * (d + 1))
                            t = tm[:, 8 * d:8 * d + 8, :].rearrange("p q (i c) -> p q i c", c=2 * b)[:, :, :, old]
                            v = ps[:, d, :].rearrange("p (q i c) -> p q i c", q=8, c=b)
                            vec.tensor_tensor(t, t, v, ALU.subtract).then_inc(tup.sem, 1)
                    for d in range(2):
                        vec.wait_ge(ups.sem, ups.at(l, 2 * w + d + 1))
                        bt = beta[:, :, 4 * d + 2 * w:4 * d + 2 * w + 2]
                        vec.tensor_tensor(
                            ub[:, 8 * d:8 * d + 8, :].rearrange("p (t e) n -> p t e n", e=2),
                            ps[:, d, :].rearrange("p (t e n) -> p t e n", t=TT, e=2),
                            bt.rearrange("p t (e o) -> p t e o", o=1).to_broadcast([P, TT, 2, HD]),
                            ALU.mult).then_inc(ube.sem, 1)
                    if w:
                        vec.wait_ge(st.sem, st.at(l, 5))
                    vec.memset(state[:, :, :], 0.0).then_inc(st.sem, 1)
                    for t in range(4):
                        n = 4 * w + t
                        vec.wait_ge(ws.sem, ws.at(l, n + 1))
                        for d in range(2):
                            tt = scan_tile(d, t)
                            vec.tensor_tensor(
                                vtmp[:, d, :, :], ps[:, 0:5:4, d * HD:(d + 1) * HD],
                                beta[:, tt, 4 * d + 2 * w:4 * d + 2 * w + 2].rearrange("p (e o) -> p e o", o=1)
                                .to_broadcast([P, 2, HD]), ALU.mult)
                        chain[0] += 1
                        vec.engine_nop().then_inc(s_vec, 1)
                        vec.wait_ge(s_vec, chain[0])
                        for d in range(2):
                            tt = scan_tile(d, t)
                            last = vec.tensor_tensor(vnew[:, d, :, :], ub[:, 8 * d + 2 * tt:8 * d + 2 * tt + 2, :],
                                                     vtmp[:, d, :, :], ALU.subtract)
                        last.then_inc(vn.sem, 1)
                        vec.wait_ge(op.sem, op.at(l, n + 1))
                        vec.wait_ge(gendx.sem, gendx.at(l, w + 1))
                        vec.wait_ge(st.sem, st.at(l, 5 * w + t + 1))
                        for d in range(2):
                            tt = scan_tile(d, t)
                            last = vec.tensor_scalar(state[:, d, :], state[:, d, :], g_state[:, d, tt:tt + 1], None,
                                                     ALU.mult)
                        link(last)
                        vec.wait_ge(su.sem, su.at(l, n + 1))
                        vec.tensor_tensor(state[:, :, :], state[:, :, :],
                                          ps[:, 6, 0:2 * HD].rearrange("p (d n) -> p d n", d=2),
                                          ALU.add).then_inc(st.sem, 1)
                        for d in range(2):
                            tt = scan_tile(d, t)
                            dst = oT[:, w, tt * P:(tt + 1) * P]
                            src = ps[:, 5, d * P:(d + 1) * P]
                            if t % 2 == 0:
                                last = vec.tensor_copy(dst, src)
                            else:
                                last = vec.tensor_tensor(dst, dst, src, ALU.add)
                        if t % 2 == 0:
                            link(last)
                            vec.engine_nop().then_inc(oe.sem, 1)
                        else:
                            last.then_inc(oe.sem, 1)

                for i in range(9, 11):
                    normed(i)
                vec.wait_ge(hn.sem, hn.at(l, 11))
                for i in range(2):
                    last = vec.tensor_tensor(y[:, 2 + i, 0:no], y[:, 2 + i, 0:no], oT[:, i, 0:no], ALU.mult)
                last.then_inc(ydn.sem, 1)
                for k in range(KD):
                    vec.wait_ge(yhi.sem, yhi.at(l, k + 1))
                    vec.tensor_tensor(a_lo[:, KD + k, 0:no], y[:, k, 0:no], a_hi[:, KD + k, 0:no].bitcast(F32),
                                      ALU.subtract).then_inc(ylo.sem, 1)

                bm = b0 + N_PROJ

                def turn(i, first=False):
                    for j in range(4):
                        lower(j, bm + 4 * i + j)
                        if j == 0 and not first:
                            merge_ops(i - 1)
                        if j == 1 and not first:
                            merge_low(i - 1)

                def merge_ops(i):
                    vec.wait_ge(s_pe, bm + 4 * i + 4)
                    vec.wait_ge(sgm.sem, sgm.before[l] + 3 * i + 3)
                    g0, g1, g2 = buf_a[:, 0, 0:no], buf_a[:, 1, 0:no], buf_b[:, 1, 0:no]
                    vec.tensor_tensor(rms[:, 0:no], g0, ps[:, 3, 0:no], ALU.mult)
                    vec.tensor_tensor(inv[:, 0:no], g1, ps[:, 4, 0:no], ALU.mult)
                    loop_link(i, 0, vec.tensor_tensor(g2, g2, ps[:, 5, 0:no], ALU.mult))
                    loop_link(i, 1, vec.tensor_tensor(rms[:, 0:no], rms[:, 0:no], inv[:, 0:no], ALU.add))
                    vec.tensor_tensor(buf_b[:, 0, 0:no], rms[:, 0:no], g2, ALU.add).then_inc(mg.sem, 1)

                merge_chain = chain[0]

                def loop_link(i, j, ins):
                    ins.then_inc(s_vec, 1)
                    vec.wait_ge(s_vec, merge_chain + 2 * i + j + 1)

                def merge_low(i):
                    vec.wait_ge(mhi.sem, mhi.before[l] + i + 1)
                    vec.tensor_tensor(a_lo[:, i, 0:no], buf_b[:, 0, 0:no], a_hi[:, i, 0:no].bitcast(F32),
                                      ALU.subtract).then_inc(mlo.sem, 1)

                turn(0, first=True)
                with vec.Fori(1, KD) as i:
                    turn(i)
                merge_ops(KD - 1)
                merge_low(KD - 1)
                chain[0] += 2 * KD
                bo = bm + 4 * KD

                for i in range(KD):
                    lower(i % RAW, bo + i)
                    if i:
                        vec.wait_ge(s_pe, bo + i)
                        add_to_x(i - 1, 6 * ((i - 1) % 2), no, l, 1).then_inc(outd.sem, 1)
                vec.wait_ge(s_pe, bo + KD)
                add_to_x(KD - 1, 6, no, l, 1).then_inc(outd.sem, 1)
                vec.engine_nop().then_inc(s_xr, 1)

            modulations(0, 0, 3, ADA_FIRST)
            norm(0, TOK)
            ffn(0)
            modulations(0, 3, 9, ADA_FIRST + 60)
            norm(1, TOK)
            mixer_vec(0)
            norm(2, TOK)
            ffn(1)
            modulations(1, 0, 9, 2 * ADA)
            norm(3, TOK)
            ffn(2)
            norm(4, TOK)
            mixer_vec(1)
            norm(5, LAT)
            ffn(3)
            norm(6, LAT, final=True)

        @block.tensor
        def _(pe):
            def ada_tile(t, w):
                for k in range(KD):
                    last = pe.matmul(mod_ps[:, t, :], w[:, k * P:(k + 1) * P], c_act[:, k, :],
                                     start=(k == 0), stop=(k == KD - 1))
                last.then_inc(s_adad, 1)

            pe.wait_ge(s_cact, 1)
            for t in range(ADA_FIRST):
                if t < ADA_BIG:
                    if t % KD == 0:
                        pe.wait_ge(s_first[t // KD], 16)
                    ada_tile(t, ada_first[:, t, :])
                else:
                    pe.wait_ge(s_ada[t % 2], 16)
                    ada_tile(t, ada[:, t % 2, :])

            def norm(s, n):
                if s == 0:
                    pe.wait_ge(s_set, 3)
                for k in range(KD):
                    pe.wait_ge(s_sq, KD * s + k + 1)
                    ins = pe.matmul(ps[:, 6, 0:n], ones[:, :], buf_a[:, k % 2, 0:n], start=(k == 0), stop=(k == KD - 1))
                    if k < KD - 1:
                        ins.then_inc(s_squ, 1)
                    else:
                        ins.then_inc(s_sum, 1)

            def products(out, rows_hi, rows_lo, j, k, i, n, first, last):
                wh, wl = w_hi[:, j % SPLIT, k * P:(k + 1) * P], w_lo[:, j % SPLIT, k * P:(k + 1) * P]
                pe.matmul(out, wh, rows_hi[:, i, 0:n], start=first, stop=False)
                pe.matmul(out, wh, rows_lo[:, i, 0:n], start=False, stop=False)
                return pe.matmul(out, wl, rows_hi[:, i, 0:n], start=False, stop=last)

            def dense(j, b, bank, n, hi=h_hi, lo=h_lo, at=0):
                pe.wait_ge(s_lo, b + 1)
                for k in range(KD):
                    ins = products(ps[:, bank, 0:n], hi, lo, j, k, at + k, n, k == 0, k == KD - 1)
                return ins

            def dense_tokens(j, b, bank, n):
                pe.wait_ge(s_lo, b + 1)
                for t in range(n // P):
                    out, cols = ps[:, bank, t * P:(t + 1) * P], slice(t * P, (t + 1) * P)
                    for k in range(KD):
                        wh, wl = w_hi[:, j % SPLIT, k * P:(k + 1) * P], w_lo[:, j % SPLIT, k * P:(k + 1) * P]
                        pe.matmul(out, h_hi[:, k, cols], wh, start=(k == 0), stop=False)
                        pe.matmul(out, h_lo[:, k, cols], wh, start=False, stop=False)
                        ins = pe.matmul(out, h_hi[:, k, cols], wl, start=False, stop=(k == KD - 1))
                return ins

            def ffn(f):
                n, s = n_tok(f), FFN_STAGE[f]
                b0, p0 = FFN_BASE[f], f * KF
                pe.wait_ge(s_h, KD * s + KD)
                t0, per = ffn_ada(f, False)

                def up(it, first=False):
                    for j in range(2):
                        q = 2 * it + j
                        if not first:
                            pe.wait_ge(s_mul, p0 + q - 1)
                        for m in range(2):
                            dense(2 * j + m, b0 + 2 * q + m, 2 * j + m, n).then_inc(s_pe, 1)
                        if per:
                            for m in range(2):
                                pe.wait_ge(s_ada[m], 8 * (t0 - ADA_BIG) + 16 * (2 * it + j + 1))
                                ada_tile(t0 + 4 * it + 2 * j + m, ada[:, m, :])
                if f == 0:
                    up(0, first=True)
                with pe.Fori(1 if f == 0 else 0, KF // 2) as it:
                    up(it)
                pe.wait_ge(s_alo, p0 + KF)
                t0, per = ffn_ada(f, True)

                def down(it, j):
                    i = 2 * it + j
                    if not (f == 0 and isinstance(it, int)):
                        pe.wait_ge(s_down, KD * f + i - 1)
                    for m, (k0, k1) in enumerate(CHUNKS):
                        pe.wait_ge(s_lo, b0 + 2 * KF + 4 * i + m + 1)
                        for k in range(k0, k1):
                            ins = products(ps[:, 4 + j, 0:n], a_hi, a_lo, m, k - k0, k, n, k == 0, k == KF - 1)
                        ins.then_inc(s_pe, 1)
                    if per:
                        for m in range(2):
                            pe.wait_ge(s_ada[m], 8 * (t0 - ADA_BIG) + 16 * (i + 1))
                            ada_tile(t0 + 2 * i + m, ada[:, m, :])
                down(0, 0)
                down(0, 1)
                with pe.Fori(1, KD // 2) as it:
                    down(it, 0)
                    down(it, 1)

            def mixer_pe(l):
                b0, no = MIX_BASE[l], (TOK, LAT)[l]
                pe.wait_ge(s_h, KD * MIX_STAGE[l] + KD)
                pe.wait_ge(bal.sem, bal.at(l, 1))
                for t in range(TT):
                    out, cols = ps[:, 6, t * 16:(t + 1) * 16], slice(t * P, (t + 1) * P)
                    for k in range(KD):
                        wh, wl = ba_hi[:, k * 16:(k + 1) * 16], ba_lo[:, k * 16:(k + 1) * 16]
                        pe.matmul(out, h_hi[:, k, cols], wh, start=(k == 0), stop=False)
                        pe.matmul(out, h_lo[:, k, cols], wh, start=False, stop=False)
                        ins = pe.matmul(out, h_hi[:, k, cols], wl, start=False, stop=(k == KD - 1))
                ins.then_inc(bap.sem, 1)
                for n in range(N_PROJ):
                    if n >= 2:
                        pe.wait_ge(evac.sem, evac.at(l, n - 1))
                    tok = TOK if n < 8 else no
                    make = dense_tokens if 7 <= n < 10 else dense
                    make(n, b0 + n, n % 2, tok).then_inc(s_pe, 1)

                def head_sum(i, n, after):
                    pe.wait_ge(hsq.sem, hsq.at(l, i + 1))
                    if after is not None:
                        pe.wait_ge(hrt.sem, hrt.at(l, after))
                    pe.matmul(ps[:, i % 2, 0:n], head_ones, buf_a[:, i % 2, 0:n], start=True,
                              stop=True).then_inc(hsum.sem, 1)

                def rotate(i):
                    pe.wait_ge(hn.sem, hn.at(l, i + 1))
                    if i >= 6:
                        pe.wait_ge(rop.sem, rop.at(l, i - 5))
                    src = kT[:, 0:LAT] if i == 4 else y[:, i - 1, 0:LAT]
                    pe.matmul(ps[:, 2 + i % 2, 0:LAT], swap, src, start=True, stop=True).then_inc(swp.sem, 1)

                pe.wait_ge(evac.sem, evac.at(l, N_PROJ))
                for i in range(9):
                    head_sum(i, TOK if i < 5 else no, i - 1 if i >= 2 else None)
                    if i - 1 >= 4:
                        rotate(i - 1)
                rotate(8)

                pe.wait_ge(s_pm, 32 * (l + 1))
                for s in range(no // LAT):
                    if s:
                        pe.wait_ge(pl2.sem, pl2.at(l, s))
                    for g in range(4):
                        r = slice((g % 2) * HD, (g % 2 + 1) * HD)
                        for kt in range(2):
                            ins = pe.matmul(ps[r, 4, (g // 2) * LAT:(g // 2 + 1) * LAT],
                                            pool_nat[:, 2 * s + kt, g * HD:(g + 1) * HD], pool_mats[:, kt, g, :],
                                            start=(kt == 0), stop=(kt == 1))
                    ins.then_inc(pl1.sem, 1)
                    pe.wait_ge(pl2.sem, pl2.at(l, s + 1))
                    if s:
                        pe.wait_ge(pl4.sem, pl4.at(l, s))
                    for g in range(4):
                        r = slice((g % 2) * HD, (g % 2 + 1) * HD)
                        ins = pe.matmul(ps[r, 5, (g // 2) * LAT:(g // 2 + 1) * LAT], w_pool[r, g // 2, :],
                                        pooled[r, s, g // 2, :], start=True, stop=True)
                    ins.then_inc(pl3.sem, 1)

                N = NAT[l]

                def head_of(n):
                    h = n % 8
                    rows = slice((h // 4) * HD, (h // 4 + 1) * HD)
                    return rows, h % 4, slice((n // 8) * P, (n // 8 + 1) * P)

                def scores(n):
                    rows, t, cols = head_of(n)
                    keys = slice(0, TOK) if n < 16 else slice(LAT, TOK)
                    if n >= 2:
                        pe.wait_ge(exq.sem, exq.at(l, n - 1))
                    pe.matmul(ps[:, n % 2, keys], y[rows, 4 + t, cols], kT[rows, keys], start=True,
                              stop=True).then_inc(sco.sem, 1)

                def turn_probs(n):
                    k0 = 0 if n < 16 else 2
                    pe.wait_ge(prb.sem, prb.at(l, n + 1))
                    if n >= 2:
                        pe.wait_ge(pte.sem, pte.at(l, n - 1))
                    for k in range(k0, TT):
                        ins = pe.transpose(ps[:, 2 + n % 2, k * P:(k + 1) * P], prob[:, n % 2, k * P:(k + 1) * P], ident)
                    ins.then_inc(ptr.sem, 1)

                def weigh(n):
                    rows, _, _ = head_of(n)
                    k0 = 0 if n < 16 else 2
                    pe.wait_ge(pte.sem, pte.at(l, n + 1))
                    if n >= 2:
                        pe.wait_ge(ate.sem, ate.at(l, n - 1))
                    else:
                        pe.wait_ge(pl4.sem, pl4.at(l, no // LAT))
                    for k in range(k0, TT):
                        ins = pe.matmul(ps[rows, 4 + n % 2, 0:P], v_nat[:, k, rows], probT[:, n % 2, k * P:(k + 1) * P],
                                        start=(k == k0), stop=(k == TT - 1))
                    ins.then_inc(att.sem, 1)

                pe.wait_ge(rop.sem, rop.at(l, 5))
                for n in range(N + 2):
                    if n < N:
                        scores(n)
                    if 1 <= n <= N:
                        turn_probs(n - 1)
                    if n >= 2:
                        weigh(n - 2)

                pe.wait_ge(ate.sem, ate.at(l, N))
                for j in range(4):
                    src = qkvT[:, 2 + j, :]
                    if j >= 2:
                        pe.wait_ge(nte.sem, nte.at(l, j - 1))
                    for t in range(TT):
                        ins = pe.transpose(ps[:, j % 2, t * P:(t + 1) * P], src[:, t * P:(t + 1) * P], ident)
                    ins.then_inc(ntp.sem, 1)
                pe.wait_ge(gdy.sem, gdy.at(l, 1))
                for d in range(2):
                    ins = pe.matmul(ps[:, 6, d * TT * 4:(d + 1) * TT * 4], tri(d), gdt[:, :, 4 * d:4 * d + 4],
                                    start=True, stop=True)
                ins.then_inc(gcp.sem, 1)
                pe.wait_ge(nte.sem, nte.at(l, 4))
                for w in range(2):
                    for i in range(4):
                        n, d, t0 = 4 * w + i, i // 2, 2 * (i % 2)
                        if i >= 2:
                            pe.wait_ge(ega.sem, ega.at(l, n - 1))
                            pe.wait_ge(rowd.sem, rowd.at(l, n - 1))
                        for q in range(4):
                            col = 4 * d + 2 * w + q % 2
                            ins = pe.matmul(ps[:, 2 + i % 2, q * P:(q + 1) * P],
                                            gdt[:, t0 + q // 2, col:col + 1].to_broadcast([P, P]), tri(d),
                                            start=True, stop=True)
                        ins.then_inc(row.sem, 1)
                        if i < 2:
                            for q in range(4):
                                r = slice((q % 2) * HD, (q % 2 + 1) * HD)
                                cols = slice((t0 + q // 2) * P, (t0 + q // 2 + 1) * P)
                                pe.matmul(ps[:, 4 + q % 2, cols], qkvT[r, 2 + w, cols], qkvT[r, 2 + w, cols],
                                          start=True, stop=True)
                                ins = pe.matmul(ps[:, q % 2, cols], qkvT[r, 2 + w, cols], qkvT[r, w, cols],
                                                start=True, stop=True)
                            ins.then_inc(gram.sem, 1)
                    for d in range(2):
                        pe.wait_ge(u1.sem, u1.at(l, 4 * w + 4))
                        for q in range(8):
                            ins = pe.transpose(ps[:, 2 + 2 * d + q // 4, (q % 4) * P:(q % 4 + 1) * P],
                                               um[:, 8 * d + q, :], ident)
                        ins.then_inc(tr0.sem, 1)
                    for i, b in enumerate(LEVELS):
                        for d in range(2):
                            n = 2 * NL * w + 2 * i + d
                            if i:
                                pe.wait_ge(tup.sem, tup.at(l, n - 1))
                            else:
                                pe.wait_ge(tr0e.sem, tr0e.at(l, 2 * w + d + 1))
                            old = slice(b * d, b * (d + 1))
                            for q in range(8):
                                t = tm[:, 8 * d + q, :].rearrange("p (i c) -> p i c", c=2 * b)[:, :, old]
                                ins = pe.matmul(ps[:, d, q * HD:(q + 1) * HD].rearrange("p (i c) -> p i c", c=b),
                                                amT[:, 8 * d + q, :], t, start=True, stop=True)
                            ins.then_inc(xps.sem, 1)
                        for d in range(2):
                            n = 2 * NL * w + 2 * i + d
                            pe.wait_ge(xmk.sem, xmk.at(l, n + 1))
                            if i:
                                pe.wait_ge(upd.sem, upd.at(l, n - 1))
                            for q in range(8):
                                ins = pe.matmul(ps[:, d, q * HD:(q + 1) * HD], um[:, 8 * d + q, :],
                                                xm[:, 8 * d + q, :], start=True, stop=True)
                            ins.then_inc(yps.sem, 1)
                        for d in range(2):
                            n = 2 * NL * w + 2 * i + d
                            pe.wait_ge(tup.sem, tup.at(l, n + 1))
                            for q in range(8):
                                ins = pe.transpose(ps[:, 2 + 2 * d + q // 4, (q % 4) * P:(q % 4 + 1) * P],
                                                   tm[:, 8 * d + q, :], ident)
                            ins.then_inc(trp.sem, 1)
                    for d in range(2):
                        pe.wait_ge(upd.sem, upd.at(l, 2 * NL * w + 2 * NL - 1 + d))
                        for q in range(8):
                            h = 2 * w + q % 2
                            ins = pe.matmul(ps[:, d, q * HD:(q + 1) * HD], um[:, 8 * d + q, :],
                                            vd_nat[:, q // 2, h * HD:(h + 1) * HD], start=True, stop=True)
                        ins.then_inc(ups.sem, 1)
                    pe.wait_ge(keg.sem, keg.at(l, w + 1))
                    for d in range(2):
                        for q in range(8):
                            r = slice((q % 2) * HD, (q % 2 + 1) * HD)
                            ins = pe.matmul(ps[r, 2 + d, (q // 2) * P:(q // 2 + 1) * P], ke[:, 8 * d + q, :],
                                            um[:, 8 * d + q, :], start=True, stop=True)
                        ins.then_inc(wps.sem, 1)
                    pe.wait_ge(wte.sem, wte.at(l, 2 * w + 2))
                    pe.wait_ge(ube.sem, ube.at(l, 2 * w + 2))
                    for t in range(4):
                        n = 4 * w + t
                        pe.wait_ge(st.sem, st.at(l, 5 * w + t + 1))
                        for d in range(2):
                            for e in range(2):
                                r = slice(e * HD, (e + 1) * HD)
                                ins = pe.matmul(ps[:, 4 * e, d * HD:(d + 1) * HD],
                                                wT[r, d, scan_tile(d, t), :], state[r, d, :], start=True, stop=True)
                        ins.then_inc(ws.sem, 1)
                        if t or w:
                            pe.wait_ge(oe.sem, oe.at(l, n))
                        pe.wait_ge(vn.sem, vn.at(l, n + 1))
                        for d in range(2):
                            tt = scan_tile(d, t)
                            for e in range(2):
                                r = slice(e * HD, (e + 1) * HD)
                                out = ps[r, 5, d * P:(d + 1) * P]
                                pe.matmul(out, state[r, d, :], q_dec[r, d, tt * P:(tt + 1) * P], start=True, stop=False)
                                ins = pe.matmul(out, vnew[:, d, e, :], qkm[:, 8 * d + 2 * tt + e, :], start=False,
                                                stop=True)
                        ins.then_inc(op.sem, 1)
                        pe.wait_ge(kds.sem, kds.at(l, n + 1))
                        for d in range(2):
                            for e in range(2):
                                r = slice(e * HD, (e + 1) * HD)
                                ins = pe.matmul(ps[r, 6, d * HD:(d + 1) * HD], kd[:, t % 2, 2 * d + e, :],
                                                vnew[:, d, e, :], start=True, stop=True)
                        ins.then_inc(su.sem, 1)
                    if w == 0:
                        pe.wait_ge(st.sem, st.at(l, 5))
                        pe.wait_ge(oe.sem, oe.at(l, 4))

                for i in range(9, 11):
                    head_sum(i, no, None)

                bm = b0 + N_PROJ
                pe.wait_ge(hrt.sem, hrt.at(l, 11))
                pe.wait_ge(ylo.sem, ylo.at(l, KD))

                def turn(i, first=False):
                    for j in range(3):
                        if not first:
                            pe.wait_ge(sgm.sem, sgm.before[l] + 3 * i - 2 + j)
                        dense(j, bm + 4 * i + j, j, no).then_inc(s_pe, 1)
                    if not first:
                        pe.wait_ge(mg.sem, mg.before[l] + i)
                    pe.wait_ge(s_lo, bm + 4 * i + 4)
                    for k in range(KD):
                        bank, lo, hi = (3, 0, 1) if k < 2 else (4, 2, 3) if k < 4 else (5, 4, 7)
                        ins = products(ps[:, bank, 0:no], a_hi, a_lo, 3, k, KD + k, no, k == lo, k == hi)
                    ins.then_inc(s_pe, 1)
                turn(0, first=True)
                with pe.Fori(1, KD) as i:
                    turn(i)
                bo = bm + 4 * KD
                pe.wait_ge(mlo.sem, mlo.at(l, KD))
                for i in range(KD):
                    if i >= 2:
                        pe.wait_ge(outd.sem, outd.at(l, i - 1))
                    dense(i, bo + i, 6 * (i % 2), no, a_hi, a_lo).then_inc(s_pe, 1)

            norm(0, TOK)
            ffn(0)
            norm(1, TOK)
            mixer_pe(0)
            norm(2, TOK)
            ffn(1)
            norm(3, TOK)
            ffn(2)
            norm(4, TOK)
            mixer_pe(1)
            norm(5, LAT)
            ffn(3)
            norm(6, LAT)


def constants():
    i = np.arange(P)
    c = np.zeros((P, N_CONST), np.float32)
    c[:, C_ID:C_ID + P] = np.eye(P)
    even = i[::2]
    c[even + 1, C_SWAP + even] = -1.0
    c[even, C_SWAP + even + 1] = 1.0
    c[:, C_HEADS:C_HEADS + P] = (i[:, None] // HD == i[None, :] // HD)
    c[:, C_TRI:C_TRI + P] = i[:, None] <= i[None, :]
    c[:, C_TRI + P:C_TRI + 2 * P] = i[:, None] >= i[None, :]
    c[even, C_M1 + even + 1] = 1.0
    c[even + 1, C_M1 + P + even] = 1.0
    j = np.arange(64)
    for n, b in enumerate(LEVELS):
        for d in range(2):
            second = i[:, None] % (2 * b) >= b
            inside = (i[:, None] // (2 * b) == j[None, :] // b) & (second if d == 0 else ~second)
            at = C_LV + (2 * n + d) * 64
            c[:, at:at + 64] = inside
    n_freq = HD // 4
    inv = (np.float32(10000.0) ** (-np.arange(n_freq, dtype=np.float32) / np.float32(n_freq))).astype(np.float32)
    t = np.arange(LAT)
    ang = np.concatenate([(t // GRID_W).astype(np.float32)[:, None] * inv, (t % GRID_W).astype(np.float32)[:, None] * inv], 1)
    ang = ang.astype(np.float64)[:, (i % HD) // 2].T
    c[:, C_COS:C_COS + LAT] = np.cos(ang)
    c[:, C_SIN:C_SIN + LAT] = np.sin(ang)
    pm = np.zeros((2, P, 4, LAT), np.float32)
    for g, w in enumerate(WINDOWS):
        lo, hi = np.clip(t - w // 2, 0, LAT), np.clip(t + w - w // 2, 0, LAT)
        m = (t[:, None] >= lo) & (t[:, None] < hi)
        pm[:, :, g, :] = (m / (hi - lo) - np.eye(LAT)).reshape(2, P, LAT)
    return c, np.ascontiguousarray(pm.transpose(1, 0, 2, 3))


def lay_out(v):
    v = {k: np.asarray(z) for k, z in v.items()}

    def blocks(w):
        return w.reshape(w.shape[0] // P, P, w.shape[1] // P, P).transpose(2, 1, 0, 3).reshape(w.shape[1] // P, P, -1)

    def chan(z):
        return z.reshape(z.shape[0], -1, P).transpose(2, 0, 1)

    tok = np.concatenate([v["x"][0], v["ctx"].reshape(CTX, D)], 0)
    out = {"xT": tok.T.reshape(KD, P, TOK).transpose(1, 0, 2)}
    out["cT"] = np.stack([v["c"][0], v["c_ctx"]], 1).reshape(KD, P, 2).transpose(1, 0, 2)
    out["w_ada"] = np.concatenate([blocks(v["w_ada"][l]) for l in range(DEPTH)])
    ups, downs = [], []
    for l in range(DEPTH):
        for n in ("1", "2"):
            u = blocks(v[f"w_ffn{n}_in"][l])
            ups.append(np.stack([u[:KF], u[KF:]], 1).reshape(2 * KF, P, KD * P))
            downs.append(blocks(v[f"w_ffn{n}_out"][l]))
    out["w_up"], out["w_down"] = np.stack(ups), np.stack(downs)
    proj, bas, merge, outs, vec, pw, rows = [], [], [], [], [], [], []
    for l in range(DEPTH):
        w = v["w_in"][l]
        heads = w[:, OFF_AQ:OFF_AK].reshape(D, 2, 4, HD).transpose(0, 2, 1, 3).reshape(D, 4 * P)
        proj.append(blocks(np.concatenate([w[:, OFF_QKV:OFF_Z], w[:, OFF_AK:OFF_AV], w[:, OFF_AV:OFF_GATE],
                                           w[:, OFF_POOL:OFF_QKV], w[:, OFF_Z:OFF_BA], heads], 1)))
        bas.append(w[:, OFF_BA:OFF_AQ].reshape(KD, P, 16).transpose(1, 0, 2).reshape(P, KD * 16))
        wb = v["w_branch"][l]
        wc = wb[2 * 256:].reshape(2, 4, HD, D).transpose(1, 0, 2, 3).reshape(4 * P, D)
        wb = blocks(np.concatenate([wb[:2 * 256], wc], 0))
        g = blocks(w[:, OFF_GATE:])
        merge.append(np.stack([g[:KD], g[KD:2 * KD], g[2 * KD:], wb], 1).reshape(4 * KD, P, KD * P))
        outs.append(blocks(v["w_out"][l]))
        cols = [chan(v["b_ada"][l][None])[:, 0], chan(v["norm_ffn1"][l][None])[:, 0],
                chan(v["norm_mix"][l][None])[:, 0], chan(v["norm_ffn2"][l][None])[:, 0],
                chan(v["pool_scale"][l][None])[:, 0],
                chan(v["dn_conv"][l]).transpose(0, 2, 1).reshape(P, 6 * TAPS)]
        cols += [np.concatenate([v[n][l], v[n][l]])[:, None] for n in ("dn_norm", "q_norm", "k_norm")]
        vec.append(np.concatenate(cols, 1))
        pw.append(v["pool_w"][l].reshape(2, 2, HD, HD).transpose(1, 2, 0, 3).reshape(P, 2, HD))
        rows.append(np.broadcast_to(np.concatenate([v["dn_dt_bias"][l].reshape(-1), v["dn_a_log"][l].reshape(-1)]), (P, 16)))
    out["w_proj"], out["w_ba"], out["w_merge"], out["w_out"] = map(np.stack, (proj, bas, merge, outs))
    out["vecs"] = np.stack(vec, 1)
    out["norm_final"] = v["norm_final"].reshape(KD, P).T
    out["w_pool"], out["ba_rows"] = np.stack(pw), np.stack(rows)
    out["consts"], out["pool_mats"] = constants()
    return {k: np.ascontiguousarray(z) for k, z in out.items()}


def kernel(**inputs):
    import concourse.bacc as bacc
    from concourse.bass_utils import run_bass_kernel_spmd

    nc = bacc.Bacc("TRN2", target_bir_lowering=False, num_devices=1)
    arrays = {f"in_{k}": z for k, z in lay_out(inputs).items()}
    aps = {k[3:]: nc.dram_tensor(k, z.shape, mybir.dt.from_np(z.dtype), kind="ExternalInput").ap()
           for k, z in arrays.items()}
    aps["out"] = nc.dram_tensor("out_y", (P, KD, LAT), F32, kind="ExternalOutput").ap()
    build_program(nc, aps)
    got = run_bass_kernel_spmd(nc, [arrays], core_ids=[0]).results[0]["out_y"]
    return np.ascontiguousarray(np.asarray(got).transpose(2, 1, 0).reshape(1, LAT, D))
```

```python
from contextlib import ExitStack

import numpy as np

import concourse.bass as bass
from concourse import mybir

F32 = mybir.dt.float32
F32R = mybir.dt.float32r
ACT = mybir.ActivationFunctionType
ALU = mybir.AluOpType
AXX = mybir.AxisListType.X

P = 128
D = 1024
KD = D // P
LAT, CTX = 256, 256
TOK = LAT + CTX
TT = TOK // P
DEPTH = 2
FF = 2816
KF = FF // P
GRID_W = 64
WINDOWS = (2, 4, 8, 16)
HEADS = 4
HD = 64
QH = 8
TAPS = 5
EPS = 1e-6
N_MOD = 9
ADA = N_MOD * KD
OFF_POOL, OFF_QKV, OFF_Z, OFF_BA, OFF_AQ, OFF_AK, OFF_AV, OFF_GATE = 0, 256, 1024, 1280, 1296, 1808, 1936, 2064

CHUNKS = ((0, 6), (6, 12), (12, 17), (17, 22))
N_FFN = 2 * KF + 4 * KD
N_PROJ = 16
N_MIX = N_PROJ + 4 * KD + KD
FFN_BASE = (0, N_FFN + N_MIX, 2 * N_FFN + N_MIX, 3 * N_FFN + 2 * N_MIX)
MIX_BASE = (N_FFN, 3 * N_FFN + N_MIX)
FFN_STAGE = (0, 2, 3, 5)
MIX_STAGE = (1, 4)
STAGE_BASE = (FFN_BASE[0], MIX_BASE[0], FFN_BASE[1], FFN_BASE[2], MIX_BASE[1], FFN_BASE[3])
RAW, SPLIT = 4, 2
ADA_FIRST = 2 * KD
ADA_DOWN = (2, 3)
ADA_REST = DEPTH * ADA - ADA_FIRST
ADA_PART = tuple(2 * KF + KD * z for z in ADA_DOWN)
assert sum(ADA_PART) == ADA_REST and ADA_PART[0] % 2 == 0
V_ADA, V_N1, V_NM, V_N2, V_PS, V_CONV, V_DN, V_QN, V_KN = 0, 72, 80, 88, 96, 98, 128, 129, 130
N_VEC = 131
LEVELS = (2, 4, 8, 16, 32, 64)
NAT = (4 * QH, 2 * QH)
N_GATE = 3 * KD
GATE_BLOCK, BRANCH_BLOCK = N_PROJ, N_PROJ + N_GATE
NORM_POINTS, DELTA_POINTS = 9, 2 * (2 * len(LEVELS) + 4)


def gate_plan(l):
    each = (3, 4)[l]
    plan = [each * i for i in range(NORM_POINTS + NAT[l] + 1)]
    rest = N_GATE * KD - plan[-1]
    return plan + [plan[-1] + rest * (i + 1) // DELTA_POINTS for i in range(DELTA_POINTS)]


def gates_finished(l, p):
    if not 0 <= p < len(gate_plan(l)) - 1:
        return range(0)
    return range(gate_plan(l)[p] // KD, gate_plan(l)[p + 1] // KD)


def delta_point(l, w, i):
    return NORM_POINTS + NAT[l] + w * DELTA_POINTS // 2 + i


C_ID, C_SWAP, C_HEADS = 0, 128, 256
N_KEEP = 384
C_TRI, C_M1, C_LV = N_KEEP, N_KEEP + 256, N_KEEP + 512
C_COS = C_LV + len(LEVELS) * 2 * 64
C_SIN = C_COS + LAT
N_CONST = C_SIN + LAT


def build_program(nc, a):
    with ExitStack() as ctx:
        def sb(name, shape, dt=F32, at=ctx):
            return at.enter_context(nc.sbuf_tensor(name, shape, dt))

        def sem(name):
            return ctx.enter_context(nc.semaphore(name))

        class Signal:

            def __init__(self, name, *per_layer):
                self.sem = sem(name)
                self.before = [sum(per_layer[:i]) for i in range(len(per_layer))]

            def at(self, layer, n):
                return self.before[layer] + n

        x = sb("x", [P, KD, TOK])
        with ExitStack() as s:
            gate_in = sb("gate_in", [P, 4, 3, TOK], at=s)
        h_hi = sb("h_hi", [P, KD, TOK], F32R)
        h_lo = sb("h_lo", [P, KD, TOK], F32R)
        raw = sb("raw", [P, RAW, KD * P])
        w_hi = sb("w_hi", [P, SPLIT, KD * P], F32R)
        w_lo = sb("w_lo", [P, SPLIT, KD * P], F32R)
        ada = sb("ada", [P, 2, KD * P])
        buf_a = sb("buf_a", [P, 2, TOK])
        buf_b = sb("buf_b", [P, 2, TOK])
        rms = sb("rms", [P, TOK])
        inv = sb("inv", [P, TOK])
        consts = sb("consts", [P, N_KEEP])
        with ExitStack() as s:
            c_wide = sb("c_wide", [P, 2, D], at=s)
        masks = sb("masks", [P, N_CONST - N_KEEP])
        pad = sb("pad", [P, 2 * D - (N_CONST - N_KEEP)])
        gate_sums = nc.dram_tensor("gate_sums", (DEPTH, N_GATE, P, TOK), F32, kind="Internal")
        ones = sb("ones", [P, P])
        eps_col = sb("eps_col", [P, 1])
        one_col = sb("one_col", [P, 1])
        vecs = sb("vecs", [P, DEPTH, N_VEC])
        nfin = sb("nfin", [P, KD])
        c_in = sb("c_in", [P, KD, 2])
        c_act = sb("c_act", [P, KD, 2])
        ada_sum = sb("ada_sum", [P, 4])
        mod_rest = sb("mod_rest", [P, ADA_REST // 2, 4])
        mod = sb("mod", [P, DEPTH, ADA, 2])
        gain = sb("gain", [P, DEPTH, 3, KD, 2])
        ident = consts[:, C_ID:C_ID + P]
        swap = consts[:, C_SWAP:C_SWAP + P]
        head_ones = consts[:, C_HEADS:C_HEADS + P]
        cos = masks[:, C_COS - N_KEEP:C_COS - N_KEEP + LAT]
        sin = masks[:, C_SIN - N_KEEP:C_SIN - N_KEEP + LAT]

        def tri(d):
            return masks[:, d * P:(d + 1) * P]

        def mask_one(d):
            return masks[:, (2 + d) * P:(3 + d) * P]

        def mask_level(i, d):
            return masks[:, C_LV - N_KEEP + (2 * i + d) * 64:C_LV - N_KEEP + (2 * i + d + 1) * 64]

        with ExitStack() as s:
            ada_first = sb("ada_first", [P, ADA_FIRST, KD * P], at=s)
        with ExitStack() as s:
            a_hi = sb("a_hi", [P, KF, TOK], F32R, at=s)
            a_lo = sb("a_lo", [P, KF, TOK], F32R, at=s)
        with ExitStack() as s:
            out_t = sb("out_t", [P, KD, LAT], at=s)
        mixer = ctx.enter_context(ExitStack())
        qkvT = sb("qkvT", [P, 6, TOK], at=mixer)
        s = ExitStack()
        pre = sb("pre", [P, 2, 2, LAT + 4], at=s)
        conv = sb("conv", [P, 2, TOK], at=s)
        kT = sb("kT", [P, TOK], at=s)
        v_nat = sb("v_nat", [P, TT, P], at=s)
        pool_nat = sb("pool_nat", [P, TT, 2 * P], at=s)
        pool_mats = sb("pool_mats", [P, 2, 4, LAT], at=s)
        pooled = sb("pooled", [P, 2, 2, LAT], at=s)
        prob = sb("prob", [P, 2, TOK], at=s)
        probT = sb("probT", [P, 2, TOK], at=s)
        ba_raw = sb("ba_raw", [P, KD * 16], at=s)
        ba_hi = sb("ba_hi", [P, KD * 16], F32R, at=s)
        ba_lo = sb("ba_lo", [P, KD * 16], F32R, at=s)
        s.close()
        s = ExitStack()
        k_nat = sb("k_nat", [P, TT, 2 * P], at=s)
        vd_nat = sb("vd_nat", [P, TT, 2 * P], at=s)
        amT = sb("amT", [P, 16, P], at=s)
        tm = sb("tm", [P, 16, P], at=s)
        um = sb("um", [P, 16, P], at=s)
        xm = sb("xm", [P, 16, HD], at=s)
        em = sb("em", [P, 2, 4, P], at=s)
        eg = sb("eg", [P, 2, 4, P], at=s)
        qkm = sb("qkm", [P, 16, P], at=s)
        q_dec = sb("q_dec", [P, 2, TOK], at=s)
        wT = sb("wT", [P, 2, TT, P], at=s)
        state = sb("state", [P, 2, HD], at=s)
        vnew = sb("vnew", [P, 2, 2, HD], at=s)
        vtmp = sb("vtmp", [P, 2, 2, HD], at=s)
        s.close()
        s = ExitStack()
        above = sb("above", [P, 15976], at=s)
        ba = sb("ba", [P, TT, 16], at=s)
        ba_rows = sb("ba_rows", [P, 16], at=s)
        beta = sb("beta", [P, TT, 8], at=s)
        gdt = sb("gdt", [P, TT, 8], at=s)
        g_abs = sb("g_abs", [P, TT, 8], at=s)
        g_log = sb("g_log", [P, TT, 8], at=s)
        neg_a = sb("neg_a", [P, 8], at=s)
        g_cum = sb("g_cum", [P, 2, TT, 4], at=s)
        g_exp = sb("g_exp", [P, 2, TT, 4], at=s)
        g_end = sb("g_end", [P, 2, TT, 4], at=s)
        g_state = sb("g_state", [P, 2, TT], at=s)
        w_pool = sb("w_pool", [P, 2, HD], at=s)
        stat = sb("stat", [P, 2, 4], at=s)
        y = sb("y", [P, KD, TOK], at=s)
        s.close()
        oT = qkvT[:, 4:6, :]
        ke = xm
        ub = em[:, :, :, :].rearrange("p a q (b n) -> p (a q b) n", b=2)
        kd = eg[:, :, :, :].rearrange("p a q n -> p a (q n)")[:, :, 0:4 * HD].rearrange("p a (q n) -> p a q n", q=4)
        ps = ctx.enter_context(nc.psum_tensor("ps", [P, 8, 512], F32))
        mod_ps = ps[:, 7, 0:2 * DEPTH * ADA].rearrange("p (t s) -> p t s", s=2)

        s_const = sem("const_loaded")
        s_gain = sem("final_gain_loaded")
        s_first = [sem(f"ada_first_loaded{i}") for i in range(4)]
        s_raw = [sem(f"raw_loaded{i}") for i in range(RAW)]
        s_ada = [sem(f"ada_loaded{i}") for i in range(2)]
        s_mixw = sem("mixer_small_loaded")
        s_bar = sem("ba_rows_loaded")
        s_pm = sem("pool_mats_loaded")
        s_out = sem("out_stored")
        s_set = sem("set_up")
        s_cact = sem("c_act_ready")
        s_adad = sem("ada_tiles_done")
        s_adc = sem("ada_sums_kept")
        s_mods = sem("mods_ready")
        s_hi = sem("w_hi_ready")
        s_lo = sem("w_lo_ready")
        s_pe = sem("blocks_done")
        s_acc = sem("squares_summed")
        s_sq = sem("last_square_ready")
        s_adu = sem("ada_used")
        s_wide = sem("c_wide_loaded")
        s_wact = sem("c_wide_ready")
        s_mask = sem("masks_loaded")
        s_gst = [sem(f"gate_sums_stored{i}") for i in range(2)]
        s_gld = [sem(f"gate_sums_loaded{i}") for i in range(4)]
        s_x = sem("x_loaded")
        s_sum = sem("sum_ready")
        s_rt = sem("root_ready")
        s_t = sem("scaled_ready")
        s_hhi = sem("h_hi_ready")
        s_h = sem("h_ready")
        s_fin = sem("final_ready")
        s_silu = sem("silu_ready")
        s_mul = sem("hidden_ready")
        s_ahi = sem("a_hi_ready")
        s_alo = sem("a_lo_ready")
        s_down = sem("down_added")
        s_act = sem("act_chain")
        s_vec = sem("vec_chain")
        s_pool = sem("pool_chain")
        bah = Signal("ba_hi_ready", 1, 1)
        bal = Signal("ba_lo_ready", 1, 1)
        bap = Signal("ba_projected", 1, 1)
        bae = Signal("ba_taken", 1, 1)
        pads = Signal("pads_zero", 1, 1)
        evac = Signal("projection_taken", N_PROJ, N_PROJ)
        cnv = Signal("conv_ready", 6, 6)
        qkv = Signal("qkv_ready", 6, 6)
        hsq = Signal("head_squares_ready", 9 + 2, 9 + 2)
        hsum = Signal("head_sums_ready", 9 + 2, 9 + 2)
        hrt = Signal("head_roots_ready", 9 + 2, 9 + 2)
        hn = Signal("head_normed", 9 + 2, 9 + 2)
        swp = Signal("swapped", 5, 5)
        rop = Signal("roped", 5, 5)
        pl1 = Signal("pooled_sum", 2, 1)
        pl2 = Signal("pooled_taken", 2, 1)
        pl3 = Signal("pool_mixed", 2, 1)
        pl4 = Signal("pool_out", 2, 1)
        sco = Signal("scores_ready", *NAT)
        nmx = Signal("max_ready", *NAT)
        exq = Signal("exp_ready", *NAT)
        prb = Signal("prob_ready", *NAT)
        ptr = Signal("prob_transposed", *NAT)
        pte = Signal("probT_ready", *NAT)
        att = Signal("attention_done", *NAT)
        ate = Signal("attention_taken", *NAT)
        bact = Signal("beta_ready", 1, 1)
        gact = Signal("log_ready", 1, 1)
        gab = Signal("dt_ready", 1, 1)
        naa = Signal("neg_a_ready", 1, 1)
        gdy = Signal("g_ready", 1, 1)
        gcp = Signal("g_summed", 1, 1)
        gct = Signal("g_cum_ready", 1, 1)
        gex = Signal("g_exp_ready", 1, 1)
        ntp = Signal("nat_transposed", 4, 4)
        nte = Signal("nat_ready", 4, 4)
        row = Signal("g_rows_ready", 8, 8)
        rowd = Signal("g_rows_read", 8, 8)
        ega = Signal("eg_ready", 8, 8)
        eax = Signal("e_ready", 8, 8)
        edn = Signal("e_used", 8, 8)
        gram = Signal("grams_ready", 4, 4)
        gend = Signal("g_end_ready", 2, 2)
        gendx = Signal("g_end_exp", 2, 2)
        u1 = Signal("u_first_ready", 8, 8)
        NL = len(LEVELS)
        tr0 = Signal("t_first_ready", 4, 4)
        tr0e = Signal("t_first_taken", 4, 4)
        xps = Signal("x_made", 4 * NL, 4 * NL)
        xmk = Signal("x_masked", 4 * NL, 4 * NL)
        yps = Signal("y_made", 4 * NL, 4 * NL)
        tup = Signal("t_updated", 4 * NL, 4 * NL)
        trp = Signal("t_transposed", 4 * NL, 4 * NL)
        upd = Signal("u_updated", 4 * NL, 4 * NL)
        ups = Signal("u_solved", 4, 4)
        ube = Signal("ub_ready", 4, 4)
        keg = Signal("ke_ready", 2, 2)
        wps = Signal("w_made", 4, 4)
        wte = Signal("wT_ready", 4, 4)
        kds = Signal("kd_ready", 8, 8)
        ws = Signal("ws_made", 8, 8)
        vn = Signal("v_new_ready", 8, 8)
        op = Signal("o_made", 8, 8)
        oe = Signal("o_taken", 8, 8)
        su = Signal("state_made", 8, 8)
        st = Signal("state_ready", 10, 10)
        ydn = Signal("y_dn_ready", 1, 1)
        yhi = Signal("y_hi_ready", KD, KD)
        ylo = Signal("y_lo_ready", KD, KD)
        gev = Signal("gate_sums_taken", N_GATE, N_GATE)
        sgm = Signal("gates_ready", KD, KD)
        mg = Signal("merged", KD, KD)
        mhi = Signal("m_hi_ready", KD, KD)
        mlo = Signal("m_lo_ready", KD, KD)
        outd = Signal("out_added", KD, KD)

        block = ctx.enter_context(nc.Block())

        def n_tok(f):
            return TOK if f < 3 else LAT

        def halves(n):
            return [(i, slice(i * LAT, (i + 1) * LAT)) for i in range(n // LAT)]

        def tile_ready(s, k):
            if s == 0:
                return s_x, 16
            if s in (2, 5):
                return outd.sem, outd.at(s // 3, k + 1)
            return s_down, KD * {1: 0, 3: 1, 4: 2, 6: 3}[s] + k + 1

        def scan_tile(d, t):
            return ((2, 3, 0, 1), (3, 2, 1, 0))[d][t]

        def mods_at(l, which):
            return ((1, 3, 3), (4, 4, 4))[l][which]

        @block.sync
        def _(sp):
            for i in range(4):
                some = slice(i * ADA_FIRST // 4, (i + 1) * ADA_FIRST // 4)
                sp.dma_start(ada_first[:, some, :], a["w_ada"][some].rearrange("t p n -> p t n")).then_inc(s_first[i], 16)

            def load(j, b, src, cols=KD * P, wait=True):
                if wait:
                    sp.wait_ge(s_lo, b - RAW + 1)
                sp.dma_start(raw[:, j, 0:cols], src).then_inc(s_raw[j], 16)

            def ffn(f):
                b0 = FFN_BASE[f]

                def up(it, wait=True):
                    for j in range(4):
                        load(j, b0 + 4 * it + j, a["w_up"][f, 4 * it + j], wait=wait)
                if f == 0:
                    up(0, wait=False)
                with sp.Fori(1 if f == 0 else 0, KF // 2) as it:
                    up(it)
                with sp.Fori(0, KD) as i:
                    for j, (k0, k1) in enumerate(CHUNKS):
                        load(j, b0 + 2 * KF + 4 * i + j, a["w_down"][f, i, :, k0 * P:k1 * P], (k1 - k0) * P)

            def mix(l):
                b0, no = MIX_BASE[l], (TOK, LAT)[l]

                def store(g):
                    sp.wait_ge(gev.sem, gev.at(l, g + 1))
                    sp.dma_start(gate_sums[l, g, :, 0:no], ada[:, g % 2, 0:no]).then_inc(s_gst[g % 2], 16)

                def gates(i):
                    for j in range(2):
                        sp.wait_ge(s_gst[j], 16 * (N_GATE // 2 * l + (3 * i + 4 - j) // 2))
                    if i >= 4:
                        sp.wait_ge(mg.sem, mg.at(l, i - 3))
                    sp.dma_start(gate_in[:, i % 4, :, 0:no],
                                 gate_sums[l, 3 * i:3 * i + 3, :, 0:no].rearrange("g p n -> p g n")
                                 ).then_inc(s_gld[i % 4], 16)

                for n in range(RAW):
                    load(n, b0 + n, a["w_proj"][l, n])
                sp.wait_ge(*tile_ready(MIX_STAGE[l], KD - 1))
                sp.dma_start(ba_raw[:, :], a["w_ba"][l]).then_inc(s_mixw, 16)
                sp.dma_start(masks[:, :], a["consts"][:, N_KEEP:N_CONST]).then_inc(s_mask, 16)
                sp.dma_start(w_pool[:, :, :], a["w_pool"][l]).then_inc(s_pm, 16)
                sp.dma_start(ba_rows[:, :], a["ba_rows"][l]).then_inc(s_bar, 16)
                sp.wait_ge(s_pm, 32 * l + 16)
                sp.dma_start(pool_mats[:, :, :, :], a["pool_mats"]).then_inc(s_pm, 16)
                for n in range(RAW, N_PROJ):
                    load(n % RAW, b0 + n, a["w_proj"][l, n])
                for g in range(N_GATE + 4):
                    src = a["w_gate"][l, g] if g < N_GATE else a["w_merge"][l, g - N_GATE]
                    load(g % RAW, b0 + GATE_BLOCK + g, src)
                    if g >= 4:
                        store(g - 4)
                sp.wait_ge(s_pe, b0 + BRANCH_BLOCK)
                for i in range(4):
                    gates(i)
                for m in range(4, 2 * KD):
                    src = a["w_merge"][l, m] if m < KD else a["w_out"][l, m - KD]
                    load(m % RAW, b0 + BRANCH_BLOCK + m, src)
                    if 4 <= m - 2 < KD:
                        gates(m - 2)

            ffn(0)
            mix(0)
            ffn(1)
            ffn(2)
            mix(1)
            ffn(3)
            sp.wait_ge(s_fin, KD)
            sp.dma_start(a["out"], out_t[:, :, :]).then_inc(s_out, 16)
            sp.wait_ge(s_out, 16)

        @block.gpsimd
        def _(pool):
            pool.memset(ones[:, :], 1.0).then_inc(s_set, 1)
            pool.memset(eps_col[:, :], EPS).then_inc(s_set, 1)
            pool.memset(one_col[:, :], 1.0).then_inc(s_set, 1)
            chain = [0]

            def link(ins):
                chain[0] += 1
                ins.then_inc(s_pool, 1)
                pool.wait_ge(s_pool, chain[0])

            def squares(s, n):
                for k in range(KD - 1):
                    pool.wait_ge(*tile_ready(s, k))
                    xk = x[:, k, 0:n]
                    if k == 0:
                        link(pool.tensor_tensor(buf_a[:, 0, 0:n], xk, xk, ALU.mult))
                        continue
                    link(pool.tensor_tensor(buf_a[:, 1, 0:n], xk, xk, ALU.mult))
                    ins = pool.tensor_tensor(buf_a[:, 0, 0:n], buf_a[:, 0, 0:n], buf_a[:, 1, 0:n], ALU.add)
                    if k < KD - 2:
                        link(ins)
                ins.then_inc(s_acc, 1)

            def load_ada(f):
                if f:
                    pool.wait_ge(*tile_ready(2, KD - 1))
                pool.dma_start(c_wide[:, :, :], a["c_rows"].rearrange("(o s) n -> o s n", o=1)
                               .to_broadcast([P, 2, D])).then_inc(s_wide, 16)
                t0 = f * ADA_PART[0]

                def load(it, wait=True):
                    for j in range(2):
                        if wait:
                            pool.wait_ge(s_adu, 2 * t0 + 4 * it + 2 * j - 2)
                        pool.dma_start(ada[:, j, :], a["w_ada_t"][t0 + 2 * it + j]).then_inc(s_ada[j], 16)
                load(0, wait=f > 0)
                with pool.Fori(1, ADA_PART[f] // 2) as it:
                    load(it)

            def mixer_pool(l):
                for w in range(2):
                    pool.wait_ge(gex.sem, gex.at(l, 1))
                    pool.wait_ge(nte.sem, nte.at(l, 4))
                    pool.wait_ge(yps.sem, yps.at(l, 2 * NL * (w + 1)))
                    for d in range(2):
                        for e in range(2):
                            h = 2 * w + e
                            last = pool.tensor_tensor(
                                ke[:, 8 * d + e:8 * d + 8:2, :], k_nat[:, :, h * HD:(h + 1) * HD],
                                g_exp[:, d, :, h:h + 1].to_broadcast([P, TT, HD]), ALU.mult)
                    last.then_inc(keg.sem, 1)
                    for t in range(4):
                        n = 4 * w + t
                        if t >= 2:
                            pool.wait_ge(su.sem, su.at(l, n - 1))
                        elif w:
                            pool.wait_ge(su.sem, su.at(l, 3 + t))
                        pool.wait_ge(gendx.sem, gendx.at(l, w + 1))
                        for d in range(2):
                            tt = scan_tile(d, t)
                            last = pool.tensor_tensor(
                                kd[:, t % 2, 2 * d:2 * d + 2, :],
                                k_nat[:, tt, 2 * w * HD:(2 * w + 2) * HD].rearrange("p (e n) -> p e n", e=2),
                                g_end[:, d, tt, 2 * w:2 * w + 2].rearrange("p (e o) -> p e o", o=1)
                                .to_broadcast([P, 2, HD]), ALU.mult)
                        last.then_inc(kds.sem, 1)

            squares(0, TOK)
            load_ada(0)
            squares(1, TOK)
            mixer_pool(0)
            squares(2, TOK)
            load_ada(1)
            squares(3, TOK)
            squares(4, TOK)
            mixer_pool(1)
            squares(5, LAT)
            squares(6, LAT)

        @block.scalar
        def _(act):
            chain = [0]

            def link(ins):
                chain[0] += 1
                ins.then_inc(s_act, 1)
                act.wait_ge(s_act, chain[0])

            act.dma_start(x[:, :, :], a["xT"]).then_inc(s_x, 16)
            act.dma_start(c_in[:, :, :], a["cT"]).then_inc(s_const, 16)
            act.wait_ge(s_const, 16)
            act.dma_start(vecs[:, :, :], a["vecs"]).then_inc(s_const, 16)
            act.dma_start(nfin[:, :], a["norm_final"]).then_inc(s_gain, 16)
            act.wait_ge(s_const, 32)
            act.dma_start(consts[:, :], a["consts"][:, 0:N_KEEP]).then_inc(s_const, 16)
            act.activation(c_act[:, :, :], c_in[:, :, :], ACT.Silu).then_inc(s_cact, 1)
            act.wait_ge(s_gain, 16)
            act.wait_ge(s_set, 3)

            def cast(j, b, cols=KD * P, free=True):
                if free:
                    act.wait_ge(s_pe, b - SPLIT + 1)
                return act.activation(w_hi[:, j % SPLIT, 0:cols], raw[:, j, 0:cols], ACT.Copy)

            def landed(j, base, it=0):
                act.wait_ge(s_raw[j], 16 * (base // RAW + 1) + 16 * it)

            def norm(s, l, which, n):
                def casts():
                    b = STAGE_BASE[s]
                    for j in range(2):
                        landed(j, b)
                        cast(j, b + j, free=b > 0).then_inc(s_hi, 1)
                if 0 < s < 6:
                    casts()
                act.wait_ge(*tile_ready(s, KD - 1))
                act.activation(buf_b[:, 1, 0:n], x[:, KD - 1, 0:n], ACT.Square).then_inc(s_sq, 1)
                act.wait_ge(s_sum, s + 1)
                act.activation(rms[:, 0:n], ps[:, 6, 0:n], ACT.Sqrt, bias=eps_col[:, 0:1],
                               scale=1.0 / D).then_inc(s_rt, 1)
                if s == 0:
                    casts()
                if which < 3:
                    act.wait_ge(s_mods, mods_at(l, which))
                for k in range(KD):
                    act.wait_ge(s_t, KD * s + k + 1)
                    if which == 3:
                        act.activation(out_t[:, k, :], buf_a[:, k % 2, 0:n], ACT.Identity,
                                       scale=nfin[:, k:k + 1]).then_inc(s_fin, 1)
                        continue
                    if k >= 2:
                        act.wait_ge(s_h, KD * s + k - 1)
                    for i, cols in halves(n):
                        last = act.activation(buf_b[:, k % 2, cols], buf_a[:, k % 2, cols], ACT.Identity,
                                              bias=mod[:, l, 3 * which * KD + k, i:i + 1],
                                              scale=gain[:, l, which, k, i:i + 1])
                    link(last)
                    act.activation(h_hi[:, k, 0:n], buf_b[:, k % 2, 0:n], ACT.Copy).then_inc(s_hhi, 1)

            def ffn(f):
                n = n_tok(f)
                b0, p0 = FFN_BASE[f], f * KF

                def finish(q, j):
                    def silu():
                        act.wait_ge(s_pe, b0 + 2 * q + 1)
                        act.activation(buf_a[:, j, 0:n], ps[:, 2 * j, 0:n], ACT.Silu).then_inc(s_silu, 1)

                    def upper():
                        act.wait_ge(s_mul, p0 + q + 1)
                        act.activation(a_hi[:, q, 0:n], buf_b[:, j, 0:n], ACT.Copy).then_inc(s_ahi, 1)
                    return silu, upper

                def pair(q, j, it=0):
                    silu, upper = finish(q - 1, 1 - j)
                    for m in range(2):
                        if m == 0:
                            silu()
                        landed(2 * j + m, b0, it)
                        cast(2 * j + m, b0 + 2 * q + m).then_inc(s_hi, 1)
                        if m == 1:
                            upper()

                if f < 2:
                    act.wait_ge(s_wide, 16 * (f + 1))
                    act.activation(c_wide[:, :, :], c_wide[:, :, :], ACT.Silu).then_inc(s_wact, 1)
                with act.Fori(0, KF // 2 - 1) as it:
                    pair(2 * it + 1, 1, it)
                    pair(2 * it + 2, 0, it + 1)
                pair(KF - 1, 1, KF // 2 - 1)
                silu, upper = finish(KF - 1, 1)
                silu()
                upper()
                with act.Fori(0, KD) as i:
                    for j, (k0, k1) in enumerate(CHUNKS):
                        landed(j, b0 + 2 * KF, i)
                        cast(j, b0 + 2 * KF + 4 * i + j, (k1 - k0) * P).then_inc(s_hi, 1)

            def mixer_act(l):
                b0, no = MIX_BASE[l], (TOK, LAT)[l]
                act.wait_ge(s_mixw, 16 * (l + 1))
                act.activation(ba_hi[:, :], ba_raw[:, :], ACT.Copy).then_inc(bah.sem, 1)

                def take(n):
                    act.wait_ge(s_pe, b0 + n + 1)
                    bank = ps[:, n % 2, :]
                    if n < 6:
                        if n >= 2:
                            act.wait_ge(cnv.sem, cnv.at(l, n - 1))
                        else:
                            act.wait_ge(pads.sem, pads.at(l, 1))
                        ins = act.activation(pre[:, n % 2, :, 2:2 + LAT],
                                             bank.rearrange("p (s n) -> p s n", s=2), ACT.Copy)
                    elif n == 6:
                        ins = act.activation(kT[:, :], bank, ACT.Copy)
                    elif n == 7:
                        ins = act.activation(v_nat[:, :, :], bank.rearrange("p (t n) -> p t n", t=TT), ACT.Copy)
                    elif n < 10:
                        ins = act.activation(pool_nat[:, 0:no // P, (n - 8) * P:(n - 7) * P],
                                             bank[:, 0:no].rearrange("p (t n) -> p t n", n=P), ACT.Copy)
                    elif n < 12:
                        ins = act.activation(y[:, 2 + n - 10, 0:no], bank[:, 0:no], ACT.Silu)
                    else:
                        ins = act.activation(y[:, 4 + n - 12, 0:no], bank[:, 0:no], ACT.Copy)
                    ins.then_inc(evac.sem, 1)

                def block(n):
                    landed(n % RAW, b0 + n - n % RAW)
                    cast(n % RAW, b0 + n).then_inc(s_hi, 1)

                def gates(p):
                    for g in gates_finished(l, p):
                        act.wait_ge(s_pe, b0 + GATE_BLOCK + g + 1)
                        if l or g >= 2:
                            act.wait_ge(s_gst[g % 2], 16 * (N_GATE // 2 * l + g // 2))
                        act.activation(ada[:, g % 2, 0:no], ps[:, 6 + g % 2, 0:no], ACT.Copy).then_inc(gev.sem, 1)
                        block(GATE_BLOCK + g + 2)

                for n in range(N_PROJ + 2):
                    if n >= 2:
                        block(n)
                    if 1 <= n < N_PROJ:
                        take(n - 1)
                    if 0 <= n - 3 < 6:
                        j = n - 3
                        act.wait_ge(cnv.sem, cnv.at(l, j + 1))
                        act.activation(qkvT[:, j, :], conv[:, j % 2, :], ACT.Silu).then_inc(qkv.sem, 1)
                    if n == N_PROJ:
                        take(N_PROJ - 1)

                act.wait_ge(bae.sem, bae.at(l, 1))
                act.activation(beta[:, :, :], ba[:, :, 0:8], ACT.Sigmoid).then_inc(bact.sem, 1)
                act.wait_ge(s_bar, 16 * (l + 1))
                act.activation(neg_a[:, :], ba_rows[:, 8:16], ACT.Exp).then_inc(naa.sem, 1)
                act.wait_ge(gab.sem, gab.at(l, 1))
                link(act.activation(g_abs[:, :, :], gdt[:, :, :], ACT.Abs))
                link(act.activation(g_log[:, :, :], g_abs[:, :, :], ACT.Exp, scale=-1.0))
                act.activation(g_abs[:, :, :], g_log[:, :, :], ACT.Ln, bias=one_col[:, 0:1]).then_inc(gact.sem, 1)

                def norm_in(l, i):
                    if i < 4:
                        return qkvT[:, i, :], TOK, 1.0
                    if i == 4:
                        return kT[:, :], TOK, 1.0 / HD
                    if i < 9:
                        return y[:, i - 1, 0:no], no, 1.0 / HD
                    return oT[:, i - 9, 0:no], no, 1.0 / HD

                def head_norms(lo, hi):
                    for i in range(lo, hi + 1):
                        if i < hi:
                            src, n, _ = norm_in(l, i)
                            if i - lo >= 2:
                                act.wait_ge(hsum.sem, hsum.at(l, i - 1))
                            act.activation(buf_a[:, i % 2, 0:n], src, ACT.Square).then_inc(hsq.sem, 1)
                        if i > lo:
                            _, n, mean = norm_in(l, i - 1)
                            act.wait_ge(hsum.sem, hsum.at(l, i))
                            if i - 1 - lo >= 2:
                                act.wait_ge(hn.sem, hn.at(l, i - 2))
                            act.activation(buf_b[:, (i - 1) % 2, 0:n], ps[:, (i - 1) % 2, 0:n], ACT.Sqrt,
                                           bias=eps_col[:, 0:1], scale=mean).then_inc(hrt.sem, 1)
                            if hi == NORM_POINTS:
                                gates(i - 1)

                act.wait_ge(qkv.sem, qkv.at(l, 6))
                act.wait_ge(evac.sem, evac.at(l, N_PROJ))
                head_norms(0, 9)

                for s in range(no // LAT):
                    act.wait_ge(pl1.sem, pl1.at(l, s + 1))
                    act.activation(pooled[:, s, :, :], ps[:, 4, :].rearrange("p (t n) -> p t n", t=2),
                                   ACT.Copy).then_inc(pl2.sem, 1)
                    act.wait_ge(pl3.sem, pl3.at(l, s + 1))
                    for t in range(2):
                        last = act.activation(y[:, t, s * LAT:(s + 1) * LAT], ps[:, 5, t * LAT:(t + 1) * LAT],
                                              ACT.Copy, scale=vecs[:, l, V_PS + t:V_PS + t + 1])
                    last.then_inc(pl4.sem, 1)

                N = NAT[l]
                for n in range(N + 1):
                    if n < N:
                        keys = slice(0, TOK) if n < 16 else slice(LAT, TOK)
                        act.wait_ge(nmx.sem, nmx.at(l, n + 1))
                        act.activation(prob[:, n % 2, keys], ps[:, n % 2, keys], ACT.Exp,
                                       bias=stat[:, n % 2, 1:2], scale=HD ** -0.5,
                                       accum_out=stat[:, n % 2, 2:3]).then_inc(exq.sem, 1)
                    if n >= 1:
                        keys = slice(0, TOK) if n - 1 < 16 else slice(LAT, TOK)
                        act.wait_ge(ptr.sem, ptr.at(l, n))
                        if n >= 3:
                            act.wait_ge(att.sem, att.at(l, n - 2))
                        act.activation(probT[:, (n - 1) % 2, keys], ps[:, 2 + (n - 1) % 2, keys],
                                       ACT.Copy).then_inc(pte.sem, 1)
                    if n < N:
                        gates(NORM_POINTS + n)

                for j in range(4):
                    act.wait_ge(ntp.sem, ntp.at(l, j + 1))
                    dst = (k_nat, vd_nat)[j // 2]
                    act.activation(dst[:, :, (j % 2) * P:(j % 2 + 1) * P],
                                   ps[:, j % 2, :].rearrange("p (t n) -> p t n", t=TT), ACT.Copy).then_inc(nte.sem, 1)
                act.wait_ge(gct.sem, gct.at(l, 1))
                act.activation(g_exp[:, :, :, :], g_cum[:, :, :, :], ACT.Exp).then_inc(gex.sem, 1)
                for w in range(2):
                    for i in range(4):
                        n = 4 * w + i
                        act.wait_ge(row.sem, row.at(l, n + 1))
                        if i >= 2:
                            act.wait_ge(edn.sem, edn.at(l, n - 1))
                        act.activation(eg[:, i % 2, :, :], ps[:, 2 + i % 2, :].rearrange("p (q n) -> p q n", q=4),
                                       ACT.Exp).then_inc(ega.sem, 1)
                        act.wait_ge(rowd.sem, rowd.at(l, n + 1))
                        act.activation(em[:, i % 2, :, :], em[:, i % 2, :, :], ACT.Exp).then_inc(eax.sem, 1)
                    act.wait_ge(gend.sem, gend.at(l, w + 1))
                    act.activation(g_end[:, :, :, 2 * w:2 * w + 2], g_end[:, :, :, 2 * w:2 * w + 2], ACT.Exp)
                    act.activation(g_state[:, :, :], g_state[:, :, :], ACT.Exp).then_inc(gendx.sem, 1)
                    for d in range(2):
                        act.wait_ge(tr0.sem, tr0.at(l, 2 * w + d + 1))
                        act.activation(tm[:, 8 * d:8 * d + 8, :],
                                       ps[:, 2 + 2 * d:4 + 2 * d, :].rearrange("p b (q n) -> p (b q) n", q=4),
                                       ACT.Copy).then_inc(tr0e.sem, 1)
                    for i, b in enumerate(LEVELS):
                        gates(delta_point(l, w, 2 * i))
                        gates(delta_point(l, w, 2 * i + 1))
                        for d in range(2):
                            n = 2 * NL * w + 2 * i + d
                            act.wait_ge(trp.sem, trp.at(l, n + 1))
                            new = slice(b * (1 - d), b * (2 - d))
                            for m in range(2):
                                q = 8 * d + 4 * m
                                u = um[:, q:q + 4, :].rearrange("p q (i c) -> p q i c", c=2 * b)
                                v = ps[:, 2 + 2 * d + m, :].rearrange("p (q i c) -> p q i c", q=4, c=2 * b)
                                last = act.activation(u[:, :, :, new], v[:, :, :, new], ACT.Copy)
                            last.then_inc(upd.sem, 1)
                    for d in range(2):
                        act.wait_ge(wps.sem, wps.at(l, 2 * w + d + 1))
                        act.activation(wT[:, d, :, :], ps[:, 2 + d, :].rearrange("p (t n) -> p t n", t=TT),
                                       ACT.Copy).then_inc(wte.sem, 1)
                    for t in range(4):
                        gates(delta_point(l, w, 2 * NL + t))
                act.wait_ge(oe.sem, oe.at(l, 8))
                head_norms(9, 11)

                act.wait_ge(ydn.sem, ydn.at(l, 1))
                act.wait_ge(ate.sem, ate.at(l, N))
                for k in range(KD):
                    act.activation(a_hi[:, KD + k, 0:no], y[:, k, 0:no], ACT.Copy).then_inc(yhi.sem, 1)

                def gate(i):
                    act.wait_ge(s_gld[i % 4], 16 * (KD // 4 * l + i // 4 + 1))
                    g = gate_in[:, i % 4, :, 0:no]
                    act.activation(g, g, ACT.Sigmoid).then_inc(sgm.sem, 1)

                gate(0)
                for i in range(KD):
                    block(BRANCH_BLOCK + i + 2)
                    if i + 1 < KD:
                        gate(i + 1)
                    act.wait_ge(mg.sem, mg.at(l, i + 1))
                    act.activation(a_hi[:, i, 0:no], buf_b[:, 0, 0:no], ACT.Copy).then_inc(mhi.sem, 1)
                for i in range(KD + 2, 2 * KD):
                    block(BRANCH_BLOCK + i)

            norm(0, 0, 0, TOK)
            ffn(0)
            norm(1, 0, 1, TOK)
            mixer_act(0)
            norm(2, 0, 2, TOK)
            ffn(1)
            norm(3, 1, 0, TOK)
            ffn(2)
            norm(4, 1, 1, TOK)
            mixer_act(1)
            norm(5, 1, 2, LAT)
            ffn(3)
            norm(6, 0, 3, LAT)

        @block.vector
        def _(vec):
            chain = [0]

            def link(ins):
                chain[0] += 1
                ins.then_inc(s_vec, 1)
                vec.wait_ge(s_vec, chain[0])

            def modulations(l, g0, g1):
                vec.wait_ge(s_const, 48)
                t0, t1 = g0 * KD, g1 * KD
                if g0 == 0 and l == 0:
                    vec.wait_ge(s_adad, ADA_FIRST)
                    src = mod_ps[:, 0:ADA_FIRST, :]
                else:
                    r0 = (ADA * l + t0 - ADA_FIRST) // 2
                    src = mod_rest[:, r0:r0 + (t1 - t0) // 2, :].rearrange("p r (t s) -> p (r t) s", s=2)
                link(vec.tensor_tensor(
                    mod[:, l, t0:t1, :], src,
                    vecs[:, l, t0:t1].rearrange("p (t o) -> p t o", o=1).to_broadcast([P, t1 - t0, 2]), ALU.add))
                for which in range(3):
                    if g0 <= 3 * which + 2 < g1 and which != 1:
                        gate = mod[:, l, (3 * which + 2) * KD:(3 * which + 3) * KD, :]
                        link(vec.tensor_scalar(gate, gate, 0.5, None, ALU.mult))
                    if not g0 <= 3 * which + 1 < g1:
                        continue
                    g = V_N1 + which * KD
                    link(vec.scalar_tensor_tensor(
                        gain[:, l, which, :, :], mod[:, l, (3 * which + 1) * KD:(3 * which + 2) * KD, :], 1.0,
                        vecs[:, l, g:g + KD].rearrange("p (t o) -> p t o", o=1).to_broadcast([P, KD, 2]),
                        ALU.add, ALU.mult))
                vec.engine_nop().then_inc(s_mods, 1)

            def norm(s, n, final=False):
                def lowers():
                    for j in range(2):
                        lower(j, STAGE_BASE[s] + j)
                if 0 < s < 6:
                    lowers()
                vec.wait_ge(s_rt, s + 1)
                link(vec.reciprocal(inv[:, 0:n], rms[:, 0:n]))
                if s == 0:
                    modulations(0, 0, 2)
                    lowers()

                def scaled(k):
                    if k >= 2:
                        vec.wait_ge(s_fin if final else s_hhi, (0 if final else KD * s) + k - 1)
                    vec.tensor_tensor(buf_a[:, k % 2, 0:n], x[:, k, 0:n], inv[:, 0:n], ALU.mult).then_inc(s_t, 1)

                scaled(0)
                for k in range(KD):
                    if k + 1 < KD:
                        scaled(k + 1)
                    if not final:
                        vec.wait_ge(s_hhi, KD * s + k + 1)
                        vec.tensor_tensor(h_lo[:, k, 0:n], buf_b[:, k % 2, 0:n], h_hi[:, k, 0:n].bitcast(F32),
                                          ALU.subtract).then_inc(s_h, 1)

            def lower(j, b, cols=KD * P):
                vec.wait_ge(s_hi, b + 1)
                vec.tensor_tensor(w_lo[:, j % SPLIT, 0:cols], raw[:, j, 0:cols],
                                  w_hi[:, j % SPLIT, 0:cols].bitcast(F32), ALU.subtract).then_inc(s_lo, 1)

            def add_to_x(k, bank, n, l, which):
                for i, cols in halves(n):
                    last = vec.scalar_tensor_tensor(x[:, k, cols], ps[:, bank, cols],
                                                    mod[:, l, (3 * which + 2) * KD + k, i:i + 1], x[:, k, cols],
                                                    ALU.mult, ALU.add)
                return last

            def ffn(f):
                n, l, which = n_tok(f), f // 2, 2 * (f % 2)
                b0, p0 = FFN_BASE[f], f * KF

                def finish(q, j):
                    vec.wait_ge(s_pe, b0 + 2 * q + 2)
                    vec.wait_ge(s_silu, p0 + q + 1)
                    vec.tensor_tensor(buf_b[:, j, 0:n], buf_a[:, j, 0:n], ps[:, 2 * j + 1, 0:n],
                                      ALU.mult).then_inc(s_mul, 1)
                    vec.wait_ge(s_ahi, p0 + q + 1)
                    vec.tensor_tensor(a_lo[:, q, 0:n], buf_b[:, j, 0:n], a_hi[:, q, 0:n].bitcast(F32),
                                      ALU.subtract).then_inc(s_alo, 1)

                ada0 = f * ADA_PART[0]

                def modulate(r):
                    for j in range(2):
                        vec.wait_ge(s_ada[j], 16 * (r + 1))
                        for i in range(2):
                            if i or j:
                                vec.wait_ge(s_adu, 4 * r + 2 * j + i)
                            vec.tensor_tensor_reduce(ps[:, 6:8, :].rearrange("p b n -> p (b n)"), ada[:, j, :],
                                                           c_wide[:, i, :], 1.0, 0.0, ALU.mult, ALU.add,
                                                           ada_sum[:, 2 * j + i:2 * j + i + 1]).then_inc(s_adu, 1)
                    vec.wait_ge(s_adu, 4 * r + 4)
                    vec.tensor_copy(mod_rest[:, r, :], ada_sum[:, :]).then_inc(s_adc, 1)
                    vec.wait_ge(s_adc, r + 1)

                def pair(q, j):
                    for m in range(2):
                        lower(2 * j + m, b0 + 2 * q + m)
                    finish(q - 1, 1 - j)
                    if f < 2:
                        modulate(ada0 // 2 + q - 1)

                if f < 2:
                    vec.wait_ge(s_wact, f + 1)
                with vec.Fori(0, KF // 2 - 1) as it:
                    pair(2 * it + 1, 1)
                    pair(2 * it + 2, 0)
                pair(KF - 1, 1)
                finish(KF - 1, 1)
                if f < 2:
                    modulate(ada0 // 2 + KF - 1)
                bd = b0 + 2 * KF

                def turn(it, j, first=False):
                    i = 2 * it + j
                    for m, (k0, k1) in enumerate(CHUNKS):
                        lower(m, bd + 4 * i + m, (k1 - k0) * P)
                        if m == 1 and not first:
                            vec.wait_ge(s_pe, bd + 4 * i)
                            add_to_x(i - 1, 5 - j, n, l, which).then_inc(s_down, 1)
                        after = ([], [(0, 3), (1, 2)], [(0, 1), (0, 3), (1, 2)])[ADA_DOWN[f] - 1 if f < 2 else 0]
                        if (j, m) in after:
                            modulate(ada0 // 2 + KF + ADA_DOWN[f] * it + after.index((j, m)))
                if f == 0:
                    modulations(0, 2, 3)
                turn(0, 0, True)
                turn(0, 1)
                with vec.Fori(1, KD // 2) as it:
                    turn(it, 0)
                    turn(it, 1)
                if f < 2:
                    modulations(f, 3 * (1 - f), 9)
                vec.wait_ge(s_pe, bd + 4 * KD)
                add_to_x(KD - 1, 5, n, l, which).then_inc(s_down, 1)

            def mixer_vec(l):
                b0, no = MIX_BASE[l], (TOK, LAT)[l]
                vec.memset(pre[:, :, :, 0:2], 0.0)
                vec.memset(pre[:, :, :, 2 + LAT:4 + LAT], 0.0).then_inc(pads.sem, 1)
                vec.wait_ge(bah.sem, bah.at(l, 1))
                vec.tensor_tensor(ba_lo[:, :], ba_raw[:, :], ba_hi[:, :].bitcast(F32),
                                  ALU.subtract).then_inc(bal.sem, 1)

                def convolve(j):
                    vec.wait_ge(evac.sem, evac.at(l, j + 1))
                    if j >= 2:
                        vec.wait_ge(qkv.sem, qkv.at(l, j - 1))
                    dst = conv[:, j % 2, :].rearrange("p (s n) -> p s n", s=2)
                    for i in range(TAPS):
                        w = vecs[:, l, V_CONV + TAPS * j + i:V_CONV + TAPS * j + i + 1]
                        src = pre[:, j % 2, :, i:i + LAT]
                        if i == 0:
                            link(vec.tensor_scalar(dst, src, w, None, ALU.mult))
                        elif i < TAPS - 1:
                            link(vec.scalar_tensor_tensor(dst, src, w, dst, ALU.mult, ALU.add))
                        else:
                            vec.scalar_tensor_tensor(dst, src, w, dst, ALU.mult, ALU.add).then_inc(cnv.sem, 1)

                def gates(p):
                    for g in gates_finished(l, p - 1):
                        n = GATE_BLOCK + g + 2
                        lower(n % RAW, b0 + n)

                for n in range(N_PROJ + 2):
                    if n >= 2:
                        lower(n % RAW, b0 + n)
                    if n == 2:
                        vec.wait_ge(bap.sem, bap.at(l, 1))
                        vec.tensor_copy(ba[:, :, :], ps[:, 6, 0:TT * 16].rearrange("p (t n) -> p t n", t=TT)
                                        ).then_inc(bae.sem, 1)
                        vec.wait_ge(s_bar, 16 * (l + 1))
                        vec.wait_ge(bae.sem, bae.at(l, 1))
                        vec.tensor_tensor(gdt[:, :, :], ba[:, :, 8:16],
                                          ba_rows[:, 0:8].rearrange("p (o n) -> p o n", o=1)
                                          .to_broadcast([P, TT, 8]), ALU.add).then_inc(gab.sem, 1)
                    if 0 <= n - 2 < 6:
                        convolve(n - 2)

                vec.wait_ge(gab.sem, gab.at(l, 1))
                vec.wait_ge(gact.sem, gact.at(l, 1))
                vec.wait_ge(naa.sem, naa.at(l, 1))
                link(vec.scalar_tensor_tensor(gdt[:, :, :], gdt[:, :, :], 0.0, g_abs[:, :, :], ALU.max, ALU.add))
                vec.scalar_tensor_tensor(gdt[:, :, :], gdt[:, :, :], -1.0,
                                         neg_a[:, :].rearrange("p (o n) -> p o n", o=1).to_broadcast([P, TT, 8]),
                                         ALU.mult, ALU.mult).then_inc(gdy.sem, 1)

                def normed(i):
                    if i < 4:
                        dst, n, f = qkvT[:, i, :], TOK, HD ** -0.5 if i < 2 else 1.0
                    elif i == 4:
                        dst, n, f = kT[:, :], TOK, vecs[:, l, V_KN:V_KN + 1]
                    elif i < 9:
                        dst, n, f = y[:, i - 1, 0:no], no, vecs[:, l, V_QN:V_QN + 1]
                    else:
                        dst, n, f = oT[:, i - 9, 0:no], no, vecs[:, l, V_DN:V_DN + 1]
                    vec.wait_ge(hrt.sem, hrt.at(l, i + 1))
                    if i:
                        vec.wait_ge(hn.sem, hn.at(l, i))
                    link(vec.reciprocal(inv[:, 0:n], buf_b[:, i % 2, 0:n]))
                    vec.scalar_tensor_tensor(dst, dst, f, inv[:, 0:n], ALU.mult, ALU.mult).then_inc(hn.sem, 1)

                def rope(i):
                    dst = kT[:, 0:LAT] if i == 4 else y[:, i - 1, 0:LAT]
                    vec.wait_ge(hn.sem, hn.at(l, i + 1))
                    vec.wait_ge(swp.sem, swp.at(l, i - 3))
                    if i > 4:
                        vec.wait_ge(rop.sem, rop.at(l, i - 4))
                    link(vec.tensor_tensor(rms[:, 0:LAT], ps[:, 2 + i % 2, 0:LAT], sin, ALU.mult))
                    link(vec.tensor_tensor(rms[:, LAT:TOK], dst, cos, ALU.mult))
                    vec.tensor_tensor(dst, rms[:, 0:LAT], rms[:, LAT:TOK], ALU.add).then_inc(rop.sem, 1)

                vec.wait_ge(s_mask, 16 * (l + 1))
                for i in range(9):
                    normed(i)
                    if i - 1 >= 4:
                        rope(i - 1)
                    gates(i)
                rope(8)

                N = NAT[l]

                def maximum(n):
                    keys = slice(0, TOK) if n < 16 else slice(LAT, TOK)
                    vec.wait_ge(sco.sem, sco.at(l, n + 1))
                    link(vec.tensor_reduce(stat[:, n % 2, 0:1], ps[:, n % 2, keys], AXX, ALU.max))
                    vec.tensor_scalar(stat[:, n % 2, 1:2], stat[:, n % 2, 0:1], -(HD ** -0.5), None,
                                      ALU.mult).then_inc(nmx.sem, 1)

                def head_of(n):
                    h = n % 8
                    rows = slice((h // 4) * HD, (h // 4 + 1) * HD)
                    return rows, h % 4, slice((n // 8) * P, (n // 8 + 1) * P)

                for n in range(N + 2):
                    if n < N:
                        maximum(n)
                    if 1 <= n <= N:
                        m = n - 1
                        keys = slice(0, TOK) if m < 16 else slice(LAT, TOK)
                        vec.wait_ge(exq.sem, exq.at(l, m + 1))
                        link(vec.reciprocal(stat[:, m % 2, 3:4], stat[:, m % 2, 2:3]))
                        vec.tensor_scalar(prob[:, m % 2, keys], prob[:, m % 2, keys], stat[:, m % 2, 3:4], None,
                                          ALU.mult).then_inc(prb.sem, 1)
                    if n >= 2:
                        m = n - 2
                        rows, t, cols = head_of(m)
                        vec.wait_ge(att.sem, att.at(l, m + 1))
                        vec.tensor_copy(y[rows, 4 + t, cols], ps[rows, 4 + m % 2, 0:P]).then_inc(ate.sem, 1)
                    if n < N:
                        gates(NORM_POINTS + n)

                vec.wait_ge(gcp.sem, gcp.at(l, 1))
                vec.tensor_copy(g_cum[:, :, :, :], ps[:, 5, 0:2 * TT * 4].rearrange("p (d t h) -> p d t h", d=2, t=TT)
                                ).then_inc(gct.sem, 1)
                vec.wait_ge(gct.sem, gct.at(l, 1))
                for w in range(2):
                    if w:
                        vec.wait_ge(su.sem, su.at(l, 4))
                    for i in range(4):
                        n, d, t0 = 4 * w + i, i // 2, 2 * (i % 2)
                        rows4 = ps[:, 2 + i % 2, :].rearrange("p (q n) -> p q n", q=4)
                        end = P - 1 if d == 0 else 0
                        vec.wait_ge(row.sem, row.at(l, n + 1))
                        vec.wait_ge(ega.sem, ega.at(l, n + 1))
                        if i >= 2:
                            vec.wait_ge(edn.sem, edn.at(l, n - 1))
                        for q in range(4):
                            g = g_cum[:, d, t0 + q // 2, 2 * w + q % 2:2 * w + q % 2 + 1]
                            vec.tensor_scalar(em[:, i % 2, q, :], rows4[:, q, :], g, 0.0, ALU.subtract, ALU.min)
                        last4 = rows4[:, :, end:end + 1].rearrange("p (t e) o -> p t (e o)", t=2)
                        link(vec.tensor_tensor(g_end[:, d, t0:t0 + 2, 2 * w:2 * w + 2], last4,
                                               g_cum[:, d, t0:t0 + 2, 2 * w:2 * w + 2], ALU.subtract))
                        for e in range(2):
                            r = slice(e * HD, (e + 1) * HD)
                            link(vec.tensor_copy(g_state[r, d, t0:t0 + 2], last4[r, :, e]))
                        vec.engine_nop().then_inc(rowd.sem, 1)
                        cols = slice(t0 * P, (t0 + 2) * P)
                        for e in range(2):
                            r = slice(e * HD, (e + 1) * HD)
                            vec.tensor_tensor(
                                q_dec[r, d, cols].rearrange("p (t n) -> p t n", t=2),
                                qkvT[r, w, cols].rearrange("p (t n) -> p t n", t=2),
                                eg[r, i % 2, e:4:2, :], ALU.mult)
                        vec.wait_ge(eax.sem, eax.at(l, n + 1))
                        vec.wait_ge(gram.sem, gram.at(l, 2 * w + 2))
                        vec.wait_ge(bact.sem, bact.at(l, 1))
                        qk = ps[:, 0:2, cols].rearrange("p e (t n) -> p t e n", t=2)
                        q0 = 8 * d + 4 * (i % 2)
                        for q in range(4):
                            bcol = d * 4 + 2 * w + q % 2
                            last = vec.scalar_tensor_tensor(
                                amT[:, q0 + q, :], ps[:, 4 + q % 2, (t0 + q // 2) * P:(t0 + q // 2 + 1) * P], beta[:, t0 + q // 2, bcol:bcol + 1],
                                em[:, i % 2, q, :], ALU.mult, ALU.mult)
                        link(last)
                        link(vec.tensor_tensor(
                            qkm[:, q0:q0 + 4, :].rearrange("p (t e) n -> p t e n", e=2), qk,
                            em[:, i % 2, :, :].rearrange("p (t e) n -> p t e n", e=2), ALU.mult))
                        link(vec.tensor_tensor(
                            um[:, q0:q0 + 4, :], amT[:, q0:q0 + 4, :],
                            mask_one(d).rearrange("p (o n) -> p o n", o=1).to_broadcast([P, 4, P]), ALU.mult))
                        vec.tensor_tensor(
                            qkm[:, q0:q0 + 4, :], qkm[:, q0:q0 + 4, :],
                            tri(d).rearrange("p (o n) -> p o n", o=1).to_broadcast([P, 4, P]),
                            ALU.mult).then_inc(edn.sem, 1)
                        vec.tensor_tensor(
                            um[:, q0:q0 + 4, :],
                            ident.rearrange("p (o n) -> p o n", o=1).to_broadcast([P, 4, P]),
                            um[:, q0:q0 + 4, :], ALU.subtract).then_inc(u1.sem, 1)
                    vec.engine_nop().then_inc(gend.sem, 1)

                    for i, b in enumerate(LEVELS):
                        for d in range(2):
                            n = 2 * NL * w + 2 * i + d
                            vec.wait_ge(xps.sem, xps.at(l, n + 1))
                            vec.tensor_tensor(
                                xm[:, 8 * d:8 * d + 8, :], ps[:, d, :].rearrange("p (q n) -> p q n", q=8),
                                mask_level(i, d).rearrange("p (o n) -> p o n", o=1).to_broadcast([P, 8, 64]),
                                ALU.mult).then_inc(xmk.sem, 1)
                        gates(delta_point(l, w, 2 * i))
                        for d in range(2):
                            n = 2 * NL * w + 2 * i + d
                            vec.wait_ge(yps.sem, yps.at(l, n + 1))
                            vec.wait_ge(tr0e.sem, tr0e.at(l, 2 * w + d + 1))
                            old = slice(b * d, b * (d + 1))
                            t = tm[:, 8 * d:8 * d + 8, :].rearrange("p q (i c) -> p q i c", c=2 * b)[:, :, :, old]
                            v = ps[:, d, :].rearrange("p (q i c) -> p q i c", q=8, c=b)
                            vec.tensor_tensor(t, t, v, ALU.subtract).then_inc(tup.sem, 1)
                        gates(delta_point(l, w, 2 * i + 1))
                    for d in range(2):
                        vec.wait_ge(ups.sem, ups.at(l, 2 * w + d + 1))
                        bt = beta[:, :, 4 * d + 2 * w:4 * d + 2 * w + 2]
                        vec.tensor_tensor(
                            ub[:, 8 * d:8 * d + 8, :].rearrange("p (t e) n -> p t e n", e=2),
                            ps[:, d, :].rearrange("p (t e n) -> p t e n", t=TT, e=2),
                            bt.rearrange("p t (e o) -> p t e o", o=1).to_broadcast([P, TT, 2, HD]),
                            ALU.mult).then_inc(ube.sem, 1)
                    if w:
                        vec.wait_ge(st.sem, st.at(l, 5))
                    vec.memset(state[:, :, :], 0.0).then_inc(st.sem, 1)
                    for t in range(4):
                        n = 4 * w + t
                        vec.wait_ge(ws.sem, ws.at(l, n + 1))
                        for d in range(2):
                            tt = scan_tile(d, t)
                            vec.tensor_tensor(
                                vtmp[:, d, :, :], ps[:, 0:5:4, d * HD:(d + 1) * HD],
                                beta[:, tt, 4 * d + 2 * w:4 * d + 2 * w + 2].rearrange("p (e o) -> p e o", o=1)
                                .to_broadcast([P, 2, HD]), ALU.mult)
                        chain[0] += 1
                        vec.engine_nop().then_inc(s_vec, 1)
                        vec.wait_ge(s_vec, chain[0])
                        for d in range(2):
                            tt = scan_tile(d, t)
                            last = vec.tensor_tensor(vnew[:, d, :, :], ub[:, 8 * d + 2 * tt:8 * d + 2 * tt + 2, :],
                                                     vtmp[:, d, :, :], ALU.subtract)
                        last.then_inc(vn.sem, 1)
                        gates(delta_point(l, w, 2 * NL + t))
                        vec.wait_ge(op.sem, op.at(l, n + 1))
                        vec.wait_ge(gendx.sem, gendx.at(l, w + 1))
                        vec.wait_ge(st.sem, st.at(l, 5 * w + t + 1))
                        for d in range(2):
                            tt = scan_tile(d, t)
                            last = vec.tensor_scalar(state[:, d, :], state[:, d, :], g_state[:, d, tt:tt + 1], None,
                                                     ALU.mult)
                        link(last)
                        vec.wait_ge(su.sem, su.at(l, n + 1))
                        vec.tensor_tensor(state[:, :, :], state[:, :, :],
                                          ps[:, 1, 0:2 * HD].rearrange("p (d n) -> p d n", d=2),
                                          ALU.add).then_inc(st.sem, 1)
                        for d in range(2):
                            tt = scan_tile(d, t)
                            dst = oT[:, w, tt * P:(tt + 1) * P]
                            src = ps[:, 5, d * P:(d + 1) * P]
                            if t % 2 == 0:
                                last = vec.tensor_copy(dst, src)
                            else:
                                last = vec.tensor_tensor(dst, dst, src, ALU.add)
                        if t % 2 == 0:
                            link(last)
                            vec.engine_nop().then_inc(oe.sem, 1)
                        else:
                            last.then_inc(oe.sem, 1)

                gates(delta_point(l, 2, 0))
                for i in range(9, 11):
                    normed(i)
                vec.wait_ge(hn.sem, hn.at(l, 11))
                for i in range(2):
                    last = vec.tensor_tensor(y[:, 2 + i, 0:no], y[:, 2 + i, 0:no], oT[:, i, 0:no], ALU.mult)
                last.then_inc(ydn.sem, 1)
                for k in range(KD):
                    vec.wait_ge(yhi.sem, yhi.at(l, k + 1))
                    vec.tensor_tensor(a_lo[:, KD + k, 0:no], y[:, k, 0:no], a_hi[:, KD + k, 0:no].bitcast(F32),
                                      ALU.subtract).then_inc(ylo.sem, 1)

                bm = b0 + BRANCH_BLOCK
                for i in range(KD):
                    vec.wait_ge(s_pe, bm + i + 1)
                    vec.wait_ge(sgm.sem, sgm.at(l, i + 1))
                    g, b = gate_in[:, i % 4, :, 0:no], 3 * (i % 2)
                    link(vec.tensor_tensor(g, g, ps[:, b:b + 3, 0:no], ALU.mult))
                    link(vec.tensor_tensor(rms[:, 0:no], g[:, 0], g[:, 1], ALU.add))
                    vec.tensor_tensor(buf_b[:, 0, 0:no], rms[:, 0:no], g[:, 2], ALU.add).then_inc(mg.sem, 1)
                    lower((i + 2) % RAW, bm + i + 2)
                    vec.wait_ge(mhi.sem, mhi.at(l, i + 1))
                    vec.tensor_tensor(a_lo[:, i, 0:no], buf_b[:, 0, 0:no], a_hi[:, i, 0:no].bitcast(F32),
                                      ALU.subtract).then_inc(mlo.sem, 1)
                bo = bm + KD
                for i in range(KD):
                    vec.wait_ge(s_pe, bo + i + 1)
                    add_to_x(i, 7 * (i % 2), no, l, 1).then_inc(outd.sem, 1)
                    if i + 2 < KD:
                        lower((i + 2) % RAW, bo + i + 2)

            norm(0, TOK)
            ffn(0)
            norm(1, TOK)
            mixer_vec(0)
            norm(2, TOK)
            ffn(1)
            norm(3, TOK)
            ffn(2)
            norm(4, TOK)
            mixer_vec(1)
            norm(5, LAT)
            ffn(3)
            norm(6, LAT, final=True)

        @block.tensor
        def _(pe):
            def ada_tile(t, w):
                for k in range(KD):
                    last = pe.matmul(mod_ps[:, t, :], w[:, k * P:(k + 1) * P], c_act[:, k, :],
                                     start=(k == 0), stop=(k == KD - 1))
                last.then_inc(s_adad, 1)

            def norm(s, n):
                if s == 0:
                    pe.wait_ge(s_set, 3)
                pe.wait_ge(s_acc, s + 1)
                pe.matmul(ps[:, 6, 0:n], ones[:, :], buf_a[:, 0, 0:n], start=True, stop=False)
                pe.wait_ge(s_sq, s + 1)
                pe.matmul(ps[:, 6, 0:n], ones[:, :], buf_b[:, 1, 0:n], start=False, stop=True).then_inc(s_sum, 1)

            def products(out, rows_hi, rows_lo, j, k, i, n, first, last):
                wh, wl = w_hi[:, j % SPLIT, k * P:(k + 1) * P], w_lo[:, j % SPLIT, k * P:(k + 1) * P]
                pe.matmul(out, wh, rows_hi[:, i, 0:n], start=first, stop=False)
                pe.matmul(out, wh, rows_lo[:, i, 0:n], start=False, stop=False)
                return pe.matmul(out, wl, rows_hi[:, i, 0:n], start=False, stop=last)

            def dense(j, b, bank, n, hi=h_hi, lo=h_lo, at=0):
                pe.wait_ge(s_lo, b + 1)
                for k in range(KD):
                    ins = products(ps[:, bank, 0:n], hi, lo, j, k, at + k, n, k == 0, k == KD - 1)
                return ins

            def dense_tokens(j, b, bank, n):
                pe.wait_ge(s_lo, b + 1)
                for t in range(n // P):
                    out, cols = ps[:, bank, t * P:(t + 1) * P], slice(t * P, (t + 1) * P)
                    for k in range(KD):
                        wh, wl = w_hi[:, j % SPLIT, k * P:(k + 1) * P], w_lo[:, j % SPLIT, k * P:(k + 1) * P]
                        pe.matmul(out, h_hi[:, k, cols], wh, start=(k == 0), stop=False)
                        pe.matmul(out, h_lo[:, k, cols], wh, start=False, stop=False)
                        ins = pe.matmul(out, h_hi[:, k, cols], wl, start=False, stop=(k == KD - 1))
                return ins

            def first_two(s, b, n):
                pe.wait_ge(s_lo, b + 2)
                for k in range(KD):
                    pe.wait_ge(s_h, KD * s + k + 1)
                    for m in range(2):
                        ins = products(ps[:, m, 0:n], h_hi, h_lo, m, k, k, n, k == 0, k == KD - 1)
                        if k == KD - 1:
                            ins.then_inc(s_pe, 1)

            def ffn(f):
                n, s = n_tok(f), FFN_STAGE[f]
                b0, p0 = FFN_BASE[f], f * KF

                def up(q, j):
                    for m in range(2):
                        dense(2 * j + m, b0 + 2 * q + m, 2 * j + m, n).then_inc(s_pe, 1)
                first_two(s, b0, n)
                up(1, 1)
                with pe.Fori(1, KF // 2) as it:
                    for j in range(2):
                        pe.wait_ge(s_mul, p0 + 2 * it + j - 1)
                        up(2 * it + j, j)
                pe.wait_ge(s_alo, p0 + KF)

                def down(it, j):
                    i = 2 * it + j
                    if not (f == 0 and isinstance(it, int)):
                        pe.wait_ge(s_down, KD * f + i - 1)
                    for m, (k0, k1) in enumerate(CHUNKS):
                        pe.wait_ge(s_lo, b0 + 2 * KF + 4 * i + m + 1)
                        for k in range(k0, k1):
                            ins = products(ps[:, 4 + j, 0:n], a_hi, a_lo, m, k - k0, k, n, k == 0, k == KF - 1)
                        ins.then_inc(s_pe, 1)
                down(0, 0)
                down(0, 1)
                with pe.Fori(1, KD // 2) as it:
                    down(it, 0)
                    down(it, 1)

            def mixer_pe(l):
                b0, no = MIX_BASE[l], (TOK, LAT)[l]
                first_two(MIX_STAGE[l], b0, TOK)
                pe.wait_ge(bal.sem, bal.at(l, 1))
                for t in range(TT):
                    out, cols = ps[:, 6, t * 16:(t + 1) * 16], slice(t * P, (t + 1) * P)
                    for k in range(KD):
                        wh, wl = ba_hi[:, k * 16:(k + 1) * 16], ba_lo[:, k * 16:(k + 1) * 16]
                        pe.matmul(out, h_hi[:, k, cols], wh, start=(k == 0), stop=False)
                        pe.matmul(out, h_lo[:, k, cols], wh, start=False, stop=False)
                        ins = pe.matmul(out, h_hi[:, k, cols], wl, start=False, stop=(k == KD - 1))
                ins.then_inc(bap.sem, 1)
                for n in range(2, N_PROJ):
                    pe.wait_ge(evac.sem, evac.at(l, n - 1))
                    tok = TOK if n < 8 else no
                    make = dense_tokens if 7 <= n < 10 else dense
                    make(n, b0 + n, n % 2, tok).then_inc(s_pe, 1)

                def gates(p):
                    plan = gate_plan(l)
                    for c in range(plan[p], plan[p + 1]):
                        g, k = divmod(c, KD)
                        b = b0 + GATE_BLOCK + g
                        if k == 0:
                            pe.wait_ge(s_lo, b + 1)
                            if g >= 2:
                                pe.wait_ge(gev.sem, gev.at(l, g - 1))
                            else:
                                pe.wait_ge(bae.sem, bae.at(l, 1))
                        ins = products(ps[:, 6 + g % 2, 0:no], h_hi, h_lo, g, k, k, no, k == 0, k == KD - 1)
                        if k == KD - 1:
                            ins.then_inc(s_pe, 1)

                def head_sum(i, n, after):
                    pe.wait_ge(hsq.sem, hsq.at(l, i + 1))
                    if after is not None:
                        pe.wait_ge(hrt.sem, hrt.at(l, after))
                    pe.matmul(ps[:, i % 2, 0:n], head_ones, buf_a[:, i % 2, 0:n], start=True,
                              stop=True).then_inc(hsum.sem, 1)

                def rotate(i):
                    pe.wait_ge(hn.sem, hn.at(l, i + 1))
                    if i >= 6:
                        pe.wait_ge(rop.sem, rop.at(l, i - 5))
                    src = kT[:, 0:LAT] if i == 4 else y[:, i - 1, 0:LAT]
                    pe.matmul(ps[:, 2 + i % 2, 0:LAT], swap, src, start=True, stop=True).then_inc(swp.sem, 1)

                pe.wait_ge(evac.sem, evac.at(l, N_PROJ))
                pe.wait_ge(s_mask, 16 * (l + 1))
                for i in range(9):
                    head_sum(i, TOK if i < 5 else no, i - 1 if i >= 2 else None)
                    if i - 1 >= 4:
                        rotate(i - 1)
                    gates(i)
                rotate(8)

                pe.wait_ge(s_pm, 32 * (l + 1))
                for s in range(no // LAT):
                    if s:
                        pe.wait_ge(pl2.sem, pl2.at(l, s))
                    for g in range(4):
                        r = slice((g % 2) * HD, (g % 2 + 1) * HD)
                        for kt in range(2):
                            ins = pe.matmul(ps[r, 4, (g // 2) * LAT:(g // 2 + 1) * LAT],
                                            pool_nat[:, 2 * s + kt, g * HD:(g + 1) * HD], pool_mats[:, kt, g, :],
                                            start=(kt == 0), stop=(kt == 1))
                    ins.then_inc(pl1.sem, 1)
                    pe.wait_ge(pl2.sem, pl2.at(l, s + 1))
                    if s:
                        pe.wait_ge(pl4.sem, pl4.at(l, s))
                    for g in range(4):
                        r = slice((g % 2) * HD, (g % 2 + 1) * HD)
                        ins = pe.matmul(ps[r, 5, (g // 2) * LAT:(g // 2 + 1) * LAT], w_pool[r, g // 2, :],
                                        pooled[r, s, g // 2, :], start=True, stop=True)
                    ins.then_inc(pl3.sem, 1)

                N = NAT[l]

                def head_of(n):
                    h = n % 8
                    rows = slice((h // 4) * HD, (h // 4 + 1) * HD)
                    return rows, h % 4, slice((n // 8) * P, (n // 8 + 1) * P)

                def scores(n):
                    rows, t, cols = head_of(n)
                    keys = slice(0, TOK) if n < 16 else slice(LAT, TOK)
                    if n >= 2:
                        pe.wait_ge(exq.sem, exq.at(l, n - 1))
                    pe.matmul(ps[:, n % 2, keys], y[rows, 4 + t, cols], kT[rows, keys], start=True,
                              stop=True).then_inc(sco.sem, 1)

                def turn_probs(n):
                    k0 = 0 if n < 16 else 2
                    pe.wait_ge(prb.sem, prb.at(l, n + 1))
                    if n >= 2:
                        pe.wait_ge(pte.sem, pte.at(l, n - 1))
                    for k in range(k0, TT):
                        ins = pe.transpose(ps[:, 2 + n % 2, k * P:(k + 1) * P], prob[:, n % 2, k * P:(k + 1) * P], ident)
                    ins.then_inc(ptr.sem, 1)

                def weigh(n):
                    rows, _, _ = head_of(n)
                    k0 = 0 if n < 16 else 2
                    pe.wait_ge(pte.sem, pte.at(l, n + 1))
                    if n >= 2:
                        pe.wait_ge(ate.sem, ate.at(l, n - 1))
                    else:
                        pe.wait_ge(pl4.sem, pl4.at(l, no // LAT))
                    for k in range(k0, TT):
                        ins = pe.matmul(ps[rows, 4 + n % 2, 0:P], v_nat[:, k, rows], probT[:, n % 2, k * P:(k + 1) * P],
                                        start=(k == k0), stop=(k == TT - 1))
                    ins.then_inc(att.sem, 1)

                pe.wait_ge(rop.sem, rop.at(l, 5))
                for n in range(N + 2):
                    if n < N:
                        scores(n)
                    if n >= 2:
                        weigh(n - 2)
                    if n < N:
                        gates(NORM_POINTS + n)
                    if 1 <= n <= N:
                        turn_probs(n - 1)

                pe.wait_ge(ate.sem, ate.at(l, N))
                for j in range(4):
                    src = qkvT[:, 2 + j, :]
                    if j >= 2:
                        pe.wait_ge(nte.sem, nte.at(l, j - 1))
                    for t in range(TT):
                        ins = pe.transpose(ps[:, j % 2, t * P:(t + 1) * P], src[:, t * P:(t + 1) * P], ident)
                    ins.then_inc(ntp.sem, 1)
                pe.wait_ge(gdy.sem, gdy.at(l, 1))
                for d in range(2):
                    ins = pe.matmul(ps[:, 5, d * TT * 4:(d + 1) * TT * 4], tri(d), gdt[:, :, 4 * d:4 * d + 4],
                                    start=True, stop=True)
                ins.then_inc(gcp.sem, 1)
                pe.wait_ge(nte.sem, nte.at(l, 4))
                pe.wait_ge(gct.sem, gct.at(l, 1))
                for w in range(2):
                    for i in range(4):
                        n, d, t0 = 4 * w + i, i // 2, 2 * (i % 2)
                        if i >= 2:
                            pe.wait_ge(ega.sem, ega.at(l, n - 1))
                            pe.wait_ge(rowd.sem, rowd.at(l, n - 1))
                        for q in range(4):
                            col = 4 * d + 2 * w + q % 2
                            ins = pe.matmul(ps[:, 2 + i % 2, q * P:(q + 1) * P],
                                            gdt[:, t0 + q // 2, col:col + 1].to_broadcast([P, P]), tri(d),
                                            start=True, stop=True)
                        ins.then_inc(row.sem, 1)
                        if i < 2:
                            for q in range(4):
                                r = slice((q % 2) * HD, (q % 2 + 1) * HD)
                                cols = slice((t0 + q // 2) * P, (t0 + q // 2 + 1) * P)
                                pe.matmul(ps[:, 4 + q % 2, cols], qkvT[r, 2 + w, cols], qkvT[r, 2 + w, cols],
                                          start=True, stop=True)
                                ins = pe.matmul(ps[:, q % 2, cols], qkvT[r, 2 + w, cols], qkvT[r, w, cols],
                                                start=True, stop=True)
                            ins.then_inc(gram.sem, 1)
                    for d in range(2):
                        pe.wait_ge(u1.sem, u1.at(l, 4 * w + 4))
                        for q in range(8):
                            ins = pe.transpose(ps[:, 2 + 2 * d + q // 4, (q % 4) * P:(q % 4 + 1) * P],
                                               um[:, 8 * d + q, :], ident)
                        ins.then_inc(tr0.sem, 1)
                    for i, b in enumerate(LEVELS):
                        for d in range(2):
                            n = 2 * NL * w + 2 * i + d
                            if i:
                                pe.wait_ge(tup.sem, tup.at(l, n - 1))
                            else:
                                pe.wait_ge(tr0e.sem, tr0e.at(l, 2 * w + d + 1))
                            old = slice(b * d, b * (d + 1))
                            for q in range(8):
                                t = tm[:, 8 * d + q, :].rearrange("p (i c) -> p i c", c=2 * b)[:, :, old]
                                ins = pe.matmul(ps[:, d, q * HD:(q + 1) * HD].rearrange("p (i c) -> p i c", c=b),
                                                amT[:, 8 * d + q, :], t, start=True, stop=True)
                            ins.then_inc(xps.sem, 1)
                        gates(delta_point(l, w, 2 * i))
                        for d in range(2):
                            n = 2 * NL * w + 2 * i + d
                            pe.wait_ge(xmk.sem, xmk.at(l, n + 1))
                            if i:
                                pe.wait_ge(upd.sem, upd.at(l, n - 1))
                            for q in range(8):
                                ins = pe.matmul(ps[:, d, q * HD:(q + 1) * HD], um[:, 8 * d + q, :],
                                                xm[:, 8 * d + q, :], start=True, stop=True)
                            ins.then_inc(yps.sem, 1)
                        gates(delta_point(l, w, 2 * i + 1))
                        for d in range(2):
                            n = 2 * NL * w + 2 * i + d
                            pe.wait_ge(tup.sem, tup.at(l, n + 1))
                            for q in range(8):
                                ins = pe.transpose(ps[:, 2 + 2 * d + q // 4, (q % 4) * P:(q % 4 + 1) * P],
                                                   tm[:, 8 * d + q, :], ident)
                            ins.then_inc(trp.sem, 1)
                    for d in range(2):
                        pe.wait_ge(upd.sem, upd.at(l, 2 * NL * w + 2 * NL - 1 + d))
                        for q in range(8):
                            h = 2 * w + q % 2
                            ins = pe.matmul(ps[:, d, q * HD:(q + 1) * HD], um[:, 8 * d + q, :],
                                            vd_nat[:, q // 2, h * HD:(h + 1) * HD], start=True, stop=True)
                        ins.then_inc(ups.sem, 1)
                    pe.wait_ge(keg.sem, keg.at(l, w + 1))
                    for d in range(2):
                        for q in range(8):
                            r = slice((q % 2) * HD, (q % 2 + 1) * HD)
                            ins = pe.matmul(ps[r, 2 + d, (q // 2) * P:(q // 2 + 1) * P], ke[:, 8 * d + q, :],
                                            um[:, 8 * d + q, :], start=True, stop=True)
                        ins.then_inc(wps.sem, 1)
                    pe.wait_ge(wte.sem, wte.at(l, 2 * w + 2))
                    pe.wait_ge(ube.sem, ube.at(l, 2 * w + 2))
                    for t in range(4):
                        n = 4 * w + t
                        pe.wait_ge(st.sem, st.at(l, 5 * w + t + 1))
                        for d in range(2):
                            for e in range(2):
                                r = slice(e * HD, (e + 1) * HD)
                                ins = pe.matmul(ps[:, 4 * e, d * HD:(d + 1) * HD],
                                                wT[r, d, scan_tile(d, t), :], state[r, d, :], start=True, stop=True)
                        ins.then_inc(ws.sem, 1)
                        gates(delta_point(l, w, 2 * NL + t))
                        if t or w:
                            pe.wait_ge(oe.sem, oe.at(l, n))
                        pe.wait_ge(vn.sem, vn.at(l, n + 1))
                        for d in range(2):
                            tt = scan_tile(d, t)
                            for e in range(2):
                                r = slice(e * HD, (e + 1) * HD)
                                out = ps[r, 5, d * P:(d + 1) * P]
                                pe.matmul(out, state[r, d, :], q_dec[r, d, tt * P:(tt + 1) * P], start=True, stop=False)
                                ins = pe.matmul(out, vnew[:, d, e, :], qkm[:, 8 * d + 2 * tt + e, :], start=False,
                                                stop=True)
                        ins.then_inc(op.sem, 1)
                        pe.wait_ge(kds.sem, kds.at(l, n + 1))
                        for d in range(2):
                            for e in range(2):
                                r = slice(e * HD, (e + 1) * HD)
                                ins = pe.matmul(ps[r, 1, d * HD:(d + 1) * HD], kd[:, t % 2, 2 * d + e, :],
                                                vnew[:, d, e, :], start=True, stop=True)
                        ins.then_inc(su.sem, 1)
                    if w == 0:
                        pe.wait_ge(st.sem, st.at(l, 5))
                        pe.wait_ge(oe.sem, oe.at(l, 4))

                for i in range(9, 11):
                    head_sum(i, no, None)

                bm = b0 + BRANCH_BLOCK
                pe.wait_ge(hrt.sem, hrt.at(l, 11))
                pe.wait_ge(ylo.sem, ylo.at(l, KD))
                for i in range(KD):
                    if i >= 2:
                        pe.wait_ge(mg.sem, mg.at(l, i - 1))
                    pe.wait_ge(s_lo, bm + i + 1)
                    for k in range(KD):
                        bank, lo, hi = (0, 0, 1) if k < 2 else (1, 2, 3) if k < 4 else (2, 4, 7)
                        ins = products(ps[:, 3 * (i % 2) + bank, 0:no], a_hi, a_lo, i, k, KD + k, no, k == lo, k == hi)
                    ins.then_inc(s_pe, 1)
                bo = bm + KD
                pe.wait_ge(mlo.sem, mlo.at(l, KD))
                for i in range(KD):
                    if i >= 2:
                        pe.wait_ge(outd.sem, outd.at(l, i - 1))
                    dense(i, bo + i, 7 * (i % 2), no, a_hi, a_lo).then_inc(s_pe, 1)

            norm(0, TOK)
            pe.wait_ge(s_cact, 1)
            for t in range(ADA_FIRST):
                if t % (ADA_FIRST // 4) == 0:
                    pe.wait_ge(s_first[t // (ADA_FIRST // 4)], 16)
                ada_tile(t, ada_first[:, t, :])
            ffn(0)
            norm(1, TOK)
            mixer_pe(0)
            norm(2, TOK)
            ffn(1)
            norm(3, TOK)
            ffn(2)
            norm(4, TOK)
            mixer_pe(1)
            norm(5, LAT)
            ffn(3)
            norm(6, LAT)


def constants():
    i = np.arange(P)
    c = np.zeros((P, N_CONST), np.float32)
    c[:, C_ID:C_ID + P] = np.eye(P)
    even = i[::2]
    c[even + 1, C_SWAP + even] = -1.0
    c[even, C_SWAP + even + 1] = 1.0
    c[:, C_HEADS:C_HEADS + P] = (i[:, None] // HD == i[None, :] // HD)
    c[:, C_TRI:C_TRI + P] = i[:, None] <= i[None, :]
    c[:, C_TRI + P:C_TRI + 2 * P] = i[:, None] >= i[None, :]
    c[even, C_M1 + even + 1] = 1.0
    c[even + 1, C_M1 + P + even] = 1.0
    j = np.arange(64)
    for n, b in enumerate(LEVELS):
        for d in range(2):
            second = i[:, None] % (2 * b) >= b
            inside = (i[:, None] // (2 * b) == j[None, :] // b) & (second if d == 0 else ~second)
            at = C_LV + (2 * n + d) * 64
            c[:, at:at + 64] = inside
    n_freq = HD // 4
    inv = (np.float32(10000.0) ** (-np.arange(n_freq, dtype=np.float32) / np.float32(n_freq))).astype(np.float32)
    t = np.arange(LAT)
    ang = np.concatenate([(t // GRID_W).astype(np.float32)[:, None] * inv, (t % GRID_W).astype(np.float32)[:, None] * inv], 1)
    ang = ang.astype(np.float64)[:, (i % HD) // 2].T
    c[:, C_COS:C_COS + LAT] = np.cos(ang)
    c[:, C_SIN:C_SIN + LAT] = np.sin(ang)
    pm = np.zeros((2, P, 4, LAT), np.float32)
    for g, w in enumerate(WINDOWS):
        lo, hi = np.clip(t - w // 2, 0, LAT), np.clip(t + w - w // 2, 0, LAT)
        m = (t[:, None] >= lo) & (t[:, None] < hi)
        pm[:, :, g, :] = (m / (hi - lo) - np.eye(LAT)).reshape(2, P, LAT)
    return c, np.ascontiguousarray(pm.transpose(1, 0, 2, 3))


def lay_out(v):
    v = {k: np.asarray(z) for k, z in v.items()}

    def blocks(w):
        return w.reshape(w.shape[0] // P, P, w.shape[1] // P, P).transpose(2, 1, 0, 3).reshape(w.shape[1] // P, P, -1)

    def chan(z):
        return z.reshape(z.shape[0], -1, P).transpose(2, 0, 1)

    tok = np.concatenate([v["x"][0], v["ctx"].reshape(CTX, D)], 0)
    out = {"xT": tok.T.reshape(KD, P, TOK).transpose(1, 0, 2)}
    out["cT"] = np.stack([v["c"][0], v["c_ctx"]], 1).reshape(KD, P, 2).transpose(1, 0, 2)
    out["w_ada"] = blocks(v["w_ada"][0][:, :ADA_FIRST * P])
    out["w_ada_t"] = v["w_ada"].transpose(0, 2, 1).reshape(DEPTH * ADA, P, D)[ADA_FIRST:]
    out["c_rows"] = np.stack([v["c"][0], v["c_ctx"]])
    ups, downs = [], []
    for l in range(DEPTH):
        for n in ("1", "2"):
            u = blocks(v[f"w_ffn{n}_in"][l])
            ups.append(np.stack([u[:KF], u[KF:]], 1).reshape(2 * KF, P, KD * P))
            downs.append(blocks(v[f"w_ffn{n}_out"][l]))
    out["w_up"], out["w_down"] = np.stack(ups), np.stack(downs)
    proj, bas, gate, merge, outs, vec, pw, rows = [], [], [], [], [], [], [], []
    for l in range(DEPTH):
        w = v["w_in"][l]
        heads = w[:, OFF_AQ:OFF_AK].reshape(D, 2, 4, HD).transpose(0, 2, 1, 3).reshape(D, 4 * P)
        proj.append(blocks(np.concatenate([w[:, OFF_QKV:OFF_Z], w[:, OFF_AK:OFF_AV], w[:, OFF_AV:OFF_GATE],
                                           w[:, OFF_POOL:OFF_QKV], w[:, OFF_Z:OFF_BA], heads], 1)))
        bas.append(w[:, OFF_BA:OFF_AQ].reshape(KD, P, 16).transpose(1, 0, 2).reshape(P, KD * 16))
        wb = v["w_branch"][l]
        wc = wb[2 * 256:].reshape(2, 4, HD, D).transpose(1, 0, 2, 3).reshape(4 * P, D)
        wb = blocks(np.concatenate([wb[:2 * 256], wc], 0))
        g = blocks(w[:, OFF_GATE:])
        gate.append(np.stack([g[:KD], g[KD:2 * KD], g[2 * KD:]], 1).reshape(N_GATE, P, KD * P))
        merge.append(wb)
        outs.append(blocks(v["w_out"][l]))
        cols = [chan(v["b_ada"][l][None])[:, 0], chan(v["norm_ffn1"][l][None])[:, 0],
                chan(v["norm_mix"][l][None])[:, 0], chan(v["norm_ffn2"][l][None])[:, 0],
                chan(v["pool_scale"][l][None])[:, 0],
                chan(v["dn_conv"][l]).transpose(0, 2, 1).reshape(P, 6 * TAPS)]
        cols += [np.concatenate([v[n][l], v[n][l]])[:, None] for n in ("dn_norm", "q_norm", "k_norm")]
        vec.append(np.concatenate(cols, 1))
        pw.append(v["pool_w"][l].reshape(2, 2, HD, HD).transpose(1, 2, 0, 3).reshape(P, 2, HD))
        rows.append(np.broadcast_to(np.concatenate([v["dn_dt_bias"][l].reshape(-1), v["dn_a_log"][l].reshape(-1)]), (P, 16)))
    out["w_proj"], out["w_ba"], out["w_gate"] = map(np.stack, (proj, bas, gate))
    out["w_merge"], out["w_out"] = np.stack(merge), np.stack(outs)
    out["vecs"] = np.stack(vec, 1)
    out["norm_final"] = v["norm_final"].reshape(KD, P).T
    out["w_pool"], out["ba_rows"] = np.stack(pw), np.stack(rows)
    out["consts"], out["pool_mats"] = constants()
    return {k: np.ascontiguousarray(z) for k, z in out.items()}


def kernel(**inputs):
    import concourse.bacc as bacc
    from concourse.bass_utils import run_bass_kernel_spmd

    nc = bacc.Bacc("TRN2", target_bir_lowering=False, num_devices=1)
    arrays = {f"in_{k}": z for k, z in lay_out(inputs).items()}
    aps = {k[3:]: nc.dram_tensor(k, z.shape, mybir.dt.from_np(z.dtype), kind="ExternalInput").ap()
           for k, z in arrays.items()}
    aps["out"] = nc.dram_tensor("out_y", (P, KD, LAT), F32, kind="ExternalOutput").ap()
    build_program(nc, aps)
    got = run_bass_kernel_spmd(nc, [arrays], core_ids=[0]).results[0]["out_y"]
    return np.ascontiguousarray(np.asarray(got).transpose(2, 1, 0).reshape(1, LAT, D))
```
